# Optimizing a Trainium2 kernel written in Bass

```python
import jax
import jax.numpy as jnp
from jax import lax
import numpy as np

D_MODEL = 2048
BATCH = 1
SEQ = 256
DEPTH = 1

HEAD_DIM = 128
NSA_HEADS = 8
NSA_KV_HEADS = 2
NSA_GROUP = NSA_HEADS // NSA_KV_HEADS
CMP_BLOCK = 32
CMP_STRIDE = 16
SEL_BLOCK = 64
N_SEL = 16
WINDOW = 512
SEL_QUERY_BLOCK = 64
FORCE_BONUS = 1e4
DSA_HEADS = 8
KV_LATENT = 256
IDX_HEADS = 4
IDX_DIM = 64
DSA_TOPK_MAX = 256
QUERY_BLOCK = 128
GMLP_GROUPS = 8
GMLP_GROUP_DIM = 128
GMLP_WIDTH = GMLP_GROUPS * GMLP_GROUP_DIM
GMLP_CHUNK = 128
N_BRANCHES = 3
BRANCH_WIDTH = D_MODEL // 2
KV_COLS = NSA_KV_HEADS * HEAD_DIM
IN_SPLITS = (NSA_HEADS * HEAD_DIM,
             KV_COLS, KV_COLS,
             KV_COLS, KV_COLS,
             KV_COLS, KV_COLS,
             NSA_HEADS * 3,
             DSA_HEADS * HEAD_DIM,
             KV_LATENT,
             IDX_HEADS * IDX_DIM,
             IDX_DIM,
             IDX_HEADS,
             2 * GMLP_WIDTH,
             N_BRANCHES * D_MODEL)
IN_COLS = sum(IN_SPLITS)
N_GROUPS = 4
EXPERTS_PER_GROUP = 4
N_EXPERTS = N_GROUPS * EXPERTS_PER_GROUP
EXPERT_TOPK = 2
D_EXPERT = 512
DEEPNORM_ALPHA = (2 * DEPTH) ** 0.25
DEEPNORM_BETA = (8 * DEPTH) ** -0.25
LN_EPS = 1e-5
NEG_BIG = -1e30

kernel_name = 'hybrid_nsa_dsa_gmlp_hmoe_deepnorm'

def _split_cols(h, sizes):
    out, start = [], 0
    for n in sizes:
        out.append(h[..., start:start + n])
        start += n
    return out

def _layer_norm(x, g, b):
    xf = x.astype(jnp.float32)
    mu = jnp.mean(xf, axis=-1, keepdims=True)
    var = jnp.mean(jnp.square(xf - mu), axis=-1, keepdims=True)
    return ((xf - mu) * lax.rsqrt(var + LN_EPS) * g + b).astype(x.dtype)

def _rms_norm(x, g):
    xf = x.astype(jnp.float32)
    return (xf * lax.rsqrt(jnp.mean(xf * xf, axis=-1, keepdims=True) + LN_EPS) * g).astype(x.dtype)

def _masked_softmax(s, valid):
    s = jnp.where(valid, s.astype(jnp.float32), NEG_BIG)
    p = jax.nn.softmax(s, axis=-1)
    return jnp.where(valid, p, 0.0)

def _alibi_slopes(n_heads):
    return 2.0 ** (-8.0 * jnp.arange(1, n_heads + 1, dtype=jnp.float32) / n_heads)

def _nsa_mixer(q, k_cmp, v_cmp, k_slc, v_slc, k_win, v_win, gates, cmp_w1, cmp_w2, cmp_pe, slopes):
    B, S = q.shape[:2]
    scale = HEAD_DIM ** -0.5
    slopes_g = slopes.reshape(NSA_KV_HEADS, NSA_GROUP)
    t_pos = jnp.arange(S)

    n_cmp = (S - CMP_BLOCK) // CMP_STRIDE + 1
    blk_idx = jnp.arange(n_cmp)[:, None] * CMP_STRIDE + jnp.arange(CMP_BLOCK)[None, :]

    def compress(x, w1, w2, pe):
        xb = x[:, blk_idx] + pe[None, None, :, None, :]
        xb = jnp.moveaxis(xb, 3, 2).reshape(B, n_cmp, NSA_KV_HEADS, CMP_BLOCK * HEAD_DIM)
        return jax.nn.gelu(xb @ w1) @ w2

    kc = compress(k_cmp, cmp_w1[0], cmp_w2[0], cmp_pe[0])
    vc = compress(v_cmp, cmp_w1[1], cmp_w2[1], cmp_pe[1])
    cmp_start = jnp.arange(n_cmp) * CMP_STRIDE
    dist_c = (t_pos[:, None] - (cmp_start + CMP_BLOCK - 1)[None, :]).astype(jnp.float32)
    s_c = jnp.einsum('bthgd,bihd->bhgti', q, kc) * scale - slopes_g[:, :, None, None] * dist_c
    p_c = _masked_softmax(s_c, dist_c >= 0)
    o_cmp = jnp.einsum('bhgti,bihd->bthgd', p_c.astype(q.dtype), vc)

    n_slc = S // SEL_BLOCK
    slc_start = jnp.arange(n_slc) * SEL_BLOCK
    overlap = ((cmp_start[:, None] < slc_start[None, :] + SEL_BLOCK)
               & (cmp_start[:, None] + CMP_BLOCK > slc_start[None, :])).astype(jnp.float32)
    imp = jnp.einsum('bhgti,ij->bhtj', p_c, overlap)
    cur = t_pos // SEL_BLOCK
    j = jnp.arange(n_slc)[None, :]
    blk_valid = j <= cur[:, None]
    forced = (j == 0) | (j == cur[:, None]) | (j == cur[:, None] - 1)
    imp = jnp.where(blk_valid, imp + jnp.where(forced, FORCE_BONUS, 0.0), NEG_BIG)
    n_sel = min(N_SEL, n_slc)
    _, sel = lax.top_k(imp, n_sel)

    ks = k_slc.reshape(B, n_slc, SEL_BLOCK, NSA_KV_HEADS, HEAD_DIM).transpose(0, 3, 1, 2, 4)
    vs = v_slc.reshape(B, n_slc, SEL_BLOCK, NSA_KV_HEADS, HEAD_DIM).transpose(0, 3, 1, 2, 4)
    qb_len = SEL_QUERY_BLOCK
    nqb = S // qb_len
    q_blocks = q.reshape(B, nqb, qb_len, NSA_KV_HEADS, NSA_GROUP, HEAD_DIM).swapaxes(0, 1)
    sel_blocks = sel.reshape(B, NSA_KV_HEADS, nqb, qb_len, n_sel).transpose(2, 0, 1, 3, 4)
    b_ix = jnp.arange(B)[:, None, None, None]
    h_ix = jnp.arange(NSA_KV_HEADS)[None, :, None, None]
    n_keys = n_sel * SEL_BLOCK

    def sel_attend(args):
        qb, sb, start = args
        kg = ks[b_ix, h_ix, sb]
        vg = vs[b_ix, h_ix, sb]
        t = start + jnp.arange(qb_len)
        s_pos = sb[..., None] * SEL_BLOCK + jnp.arange(SEL_BLOCK)
        dist = (t[None, None, :, None, None] - s_pos).astype(jnp.float32)
        s = (jnp.einsum('bqhgd,bhqnld->bhgqnl', qb, kg) * scale
             - slopes_g[None, :, :, None, None, None] * dist[:, :, None])
        p = _masked_softmax(s.reshape(B, NSA_KV_HEADS, NSA_GROUP, qb_len, n_keys),
                            (dist >= 0).reshape(B, NSA_KV_HEADS, 1, qb_len, n_keys))
        return jnp.einsum('bhgqk,bhqkd->bqhgd', p.astype(qb.dtype),
                          vg.reshape(B, NSA_KV_HEADS, qb_len, n_keys, HEAD_DIM))

    o_slc = lax.map(sel_attend, (q_blocks, sel_blocks, jnp.arange(nqb) * qb_len))
    o_slc = o_slc.swapaxes(0, 1).reshape(B, S, NSA_KV_HEADS, NSA_GROUP, HEAD_DIM)

    nwb = S // QUERY_BLOCK
    span = WINDOW + QUERY_BLOCK
    kp = jnp.pad(k_win, ((0, 0), (WINDOW, 0), (0, 0), (0, 0)))
    vp = jnp.pad(v_win, ((0, 0), (WINDOW, 0), (0, 0), (0, 0)))
    win_idx = jnp.arange(nwb)[:, None] * QUERY_BLOCK + jnp.arange(span)[None, :]
    kw = kp[:, win_idx]
    vw = vp[:, win_idx]
    t_w = jnp.arange(nwb)[:, None] * QUERY_BLOCK + jnp.arange(QUERY_BLOCK)[None, :]
    s_w = win_idx - WINDOW
    dist_w = t_w[:, :, None] - s_w[:, None, :]
    valid_w = (dist_w >= 0) & (dist_w < WINDOW) & (s_w[:, None, :] >= 0)
    qw = q.reshape(B, nwb, QUERY_BLOCK, NSA_KV_HEADS, NSA_GROUP, HEAD_DIM)
    s = (jnp.einsum('bnqhgd,bnkhd->bhgnqk', qw, kw) * scale
         - slopes_g[:, :, None, None, None] * dist_w.astype(jnp.float32))
    p = _masked_softmax(s, valid_w)
    o_win = jnp.einsum('bhgnqk,bnkhd->bnqhgd', p.astype(q.dtype), vw)
    o_win = o_win.reshape(B, S, NSA_KV_HEADS, NSA_GROUP, HEAD_DIM)

    g = jax.nn.sigmoid(gates.astype(jnp.float32)).astype(q.dtype).reshape(B, S, NSA_KV_HEADS, NSA_GROUP, 3)
    o = g[..., 0:1] * o_cmp + g[..., 1:2] * o_slc + g[..., 2:3] * o_win
    return o.reshape(B, S, NSA_HEADS * HEAD_DIM)

def _dsa_mixer(q, c_kv, q_idx, k_idx, w_idx, w_uk, w_uv, kv_norm_g, slopes):
    B, S = q.shape[:2]
    c = _rms_norm(c_kv, kv_norm_g)
    q_lat = jnp.einsum('bthd,hcd->bthc', q, w_uk) * (HEAD_DIM ** -0.5)
    topk = min(DSA_TOPK_MAX, S // 4)
    nqb = S // QUERY_BLOCK
    s_pos = jnp.arange(S)

    def blk(a):
        return a.reshape((B, nqb, QUERY_BLOCK) + a.shape[2:]).swapaxes(0, 1)

    def attend(args):
        ql, qi, wi, start = args
        t = start + jnp.arange(QUERY_BLOCK)
        rel = jax.nn.relu(jnp.einsum('bqhd,bsd->bqhs', qi, k_idx))
        score = jnp.einsum('bqhs,bqh->bqs', rel, wi).astype(jnp.float32)
        score = jnp.where(s_pos[None, None, :] <= t[None, :, None], score, -jnp.inf)
        _, sel = lax.top_k(score, topk)
        cg = jax.vmap(lambda cb, ib: cb[ib])(c, sel)
        dist = (t[None, :, None] - sel).astype(jnp.float32)
        logits = (jnp.einsum('bqhc,bqkc->bhqk', ql, cg)
                  - slopes[None, :, None, None] * dist[:, None])
        p = _masked_softmax(logits, (dist >= 0)[:, None])
        return jnp.einsum('bhqk,bqkc->bqhc', p.astype(cg.dtype), cg)

    o_lat = lax.map(attend, (blk(q_lat), blk(q_idx), blk(w_idx), jnp.arange(nqb) * QUERY_BLOCK))
    o_lat = o_lat.swapaxes(0, 1).reshape(B, S, DSA_HEADS, KV_LATENT)
    o = jnp.einsum('bthc,hcd->bthd', o_lat, w_uv)
    return o.reshape(B, S, DSA_HEADS * HEAD_DIM)

def _gmlp_mixer(uv, ln_g, ln_b, w_s, b_s):
    B, S = uv.shape[:2]
    z = jax.nn.gelu(uv)
    u, v = z[..., :GMLP_WIDTH], z[..., GMLP_WIDTH:]
    v = _layer_norm(v, ln_g, ln_b)
    nc = S // GMLP_CHUNK
    v = v.reshape(B, nc, GMLP_CHUNK, GMLP_GROUPS, GMLP_GROUP_DIM)
    causal = jnp.tril(jnp.ones((GMLP_CHUNK, GMLP_CHUNK), dtype=bool))
    w = jnp.where(causal[None], w_s, 0.0).astype(v.dtype)
    mixed = jnp.einsum('gts,bcsgd->bctgd', w, v) + b_s.T[None, None, :, :, None]
    return u * mixed.reshape(B, S, GMLP_WIDTH)

def _hier_moe(x, wg_r, bg_r, we_r, be_r, w_gate, w_up, w_down):
    B, S, D = x.shape
    xt = x.reshape(B * S, D)
    n_tok = B * S
    group_prob = jax.nn.softmax((xt @ wg_r + bg_r).astype(jnp.float32), axis=-1)
    gp, gi = lax.top_k(group_prob, 1)
    exp_logits = (xt @ we_r + be_r).astype(jnp.float32).reshape(n_tok, N_GROUPS, EXPERTS_PER_GROUP)
    in_group = exp_logits[jnp.arange(n_tok), gi[:, 0]]
    top_logits, ei = lax.top_k(in_group, EXPERT_TOPK)
    weights = gp * jax.nn.softmax(top_logits, axis=-1)
    expert_id = gi * EXPERTS_PER_GROUP + ei
    combine = jnp.sum(jax.nn.one_hot(expert_id, N_EXPERTS, dtype=jnp.float32) * weights[..., None], axis=1)
    h = jax.nn.silu(jnp.einsum('td,edf->etf', xt, w_gate)) * jnp.einsum('td,edf->etf', xt, w_up)
    h = h * combine.T[:, :, None].astype(h.dtype)
    return jnp.einsum('etf,efd->td', h, w_down).reshape(B, S, D)

def setup_inputs(seed: int = 0) -> dict:
    key = jax.random.key(seed)
    ks = jax.random.split(key, 25)

    def nrm(k, shape, scale):
        return jax.random.normal(k, shape, jnp.float32) * scale

    L, D, W = DEPTH, D_MODEL, BRANCH_WIDTH
    return {
        'x': nrm(ks[0], (BATCH, SEQ, D), 1.0),
        'w_in': nrm(ks[1], (L, D, IN_COLS), D ** -0.5),
        'cmp_w1': nrm(ks[2], (L, 2, CMP_BLOCK * HEAD_DIM, HEAD_DIM), (CMP_BLOCK * HEAD_DIM) ** -0.5),
        'cmp_w2': nrm(ks[3], (L, 2, HEAD_DIM, HEAD_DIM), HEAD_DIM ** -0.5),
        'cmp_pe': nrm(ks[4], (L, 2, CMP_BLOCK, HEAD_DIM), 0.1),
        'w_uk': nrm(ks[5], (L, DSA_HEADS, KV_LATENT, HEAD_DIM), KV_LATENT ** -0.5),
        'w_uv': nrm(ks[6], (L, DSA_HEADS, KV_LATENT, HEAD_DIM), KV_LATENT ** -0.5),
        'kv_norm_g': 1.0 + nrm(ks[7], (L, KV_LATENT), 0.01),
        'gmlp_ln_g': 1.0 + nrm(ks[8], (L, GMLP_WIDTH), 0.01),
        'gmlp_ln_b': nrm(ks[9], (L, GMLP_WIDTH), 0.01),
        'gmlp_w_s': nrm(ks[10], (L, GMLP_GROUPS, GMLP_CHUNK, GMLP_CHUNK), GMLP_CHUNK ** -0.5),
        'gmlp_b_s': 1.0 + nrm(ks[11], (L, GMLP_GROUPS, GMLP_CHUNK), 0.1),
        'w_branch': nrm(ks[12], (L, N_BRANCHES, W, D), W ** -0.5 * DEEPNORM_BETA),
        'w_out': nrm(ks[13], (L, D, D), D ** -0.5 * DEEPNORM_BETA),
        'ln1_g': 1.0 + nrm(ks[14], (L, D), 0.01),
        'ln1_b': nrm(ks[15], (L, D), 0.01),
        'router_group_w': nrm(ks[16], (L, D, N_GROUPS), D ** -0.5),
        'router_group_b': nrm(ks[17], (L, N_GROUPS), 0.01),
        'router_expert_w': nrm(ks[18], (L, D, N_EXPERTS), D ** -0.5),
        'router_expert_b': nrm(ks[19], (L, N_EXPERTS), 0.01),
        'expert_w_gate': nrm(ks[20], (L, N_EXPERTS, D, D_EXPERT), D ** -0.5),
        'expert_w_up': nrm(ks[21], (L, N_EXPERTS, D, D_EXPERT), D ** -0.5 * DEEPNORM_BETA),
        'expert_w_down': nrm(ks[22], (L, N_EXPERTS, D_EXPERT, D), D_EXPERT ** -0.5 * DEEPNORM_BETA),
        'ln2_g': 1.0 + nrm(ks[23], (L, D), 0.01),
        'ln2_b': nrm(ks[24], (L, D), 0.01),
    }

def reference(x, w_in, cmp_w1, cmp_w2, cmp_pe, w_uk, w_uv, kv_norm_g, gmlp_ln_g, gmlp_ln_b,
              gmlp_w_s, gmlp_b_s, w_branch, w_out, ln1_g, ln1_b, router_group_w, router_group_b,
              router_expert_w, router_expert_b, expert_w_gate, expert_w_up, expert_w_down,
              ln2_g, ln2_b):
    B, S, D = x.shape
    slopes = _alibi_slopes(NSA_HEADS)
    for l in range(DEPTH):
        h = x @ w_in[l]
        (q_a, k_c, v_c, k_s, v_s, k_w, v_w, g_nsa, q_b, c_kv, q_idx, k_idx, w_idx,
         uv, g_merge) = _split_cols(h, IN_SPLITS)
        kv_shape = (B, S, NSA_KV_HEADS, HEAD_DIM)
        o_a = _nsa_mixer(q_a.reshape(B, S, NSA_KV_HEADS, NSA_GROUP, HEAD_DIM),
                         k_c.reshape(kv_shape), v_c.reshape(kv_shape),
                         k_s.reshape(kv_shape), v_s.reshape(kv_shape),
                         k_w.reshape(kv_shape), v_w.reshape(kv_shape),
                         g_nsa, cmp_w1[l], cmp_w2[l], cmp_pe[l], slopes)
        o_b = _dsa_mixer(q_b.reshape(B, S, DSA_HEADS, HEAD_DIM), c_kv,
                         q_idx.reshape(B, S, IDX_HEADS, IDX_DIM), k_idx, w_idx,
                         w_uk[l], w_uv[l], kv_norm_g[l], slopes)
        o_c = _gmlp_mixer(uv, gmlp_ln_g[l], gmlp_ln_b[l], gmlp_w_s[l], gmlp_b_s[l])
        branches = jnp.stack([o_a, o_b, o_c], axis=2)
        y = jnp.einsum('bsnw,nwd->bsnd', branches, w_branch[l])
        gates = jax.nn.sigmoid(g_merge.astype(jnp.float32)).astype(x.dtype).reshape(B, S, N_BRANCHES, D)
        mixed = jnp.sum(gates * y, axis=2) @ w_out[l]
        x = _layer_norm(DEEPNORM_ALPHA * x + mixed, ln1_g[l], ln1_b[l])
        ffn = _hier_moe(x, router_group_w[l], router_group_b[l], router_expert_w[l], router_expert_b[l],
                        expert_w_gate[l], expert_w_up[l], expert_w_down[l])
        x = _layer_norm(DEEPNORM_ALPHA * x + ffn, ln2_g[l], ln2_b[l])
    return x


_drawn_inputs = setup_inputs


def setup_inputs(seed=0):
    import zlib

    import numpy as np

    out = dict(_drawn_inputs(seed))
    spreads = {}
    factors = {'cmp_pe': 8.0,
     'kv_norm_g': 8.0,
     'gmlp_ln_g': 37.055,
     'gmlp_ln_b': 64.0,
     'gmlp_b_s': 4.917,
     'ln1_g': 5.121,
     'ln1_b': 5.001,
     'router_group_b': 8.0,
     'router_expert_b': 23.328,
     'ln2_g': 191.258,
     'ln2_b': 188.638}
    for name, (base, spread) in spreads.items():
        noise = np.random.default_rng([zlib.crc32(name.encode()), seed]).standard_normal(out[name].shape)
        drawn = base * np.exp(spread * noise) if base else spread * noise
        out[name] = jnp.asarray(drawn.astype(out[name].dtype))
    for name, factor in factors.items():
        out[name] = (out[name] * factor).astype(out[name].dtype)
    return out
```

```python
from contextlib import ExitStack, contextmanager

import numpy as np

import concourse.bass as bass
from concourse import mybir

F32, F32R, I32 = mybir.dt.float32, mybir.dt.float32r, mybir.dt.int32
ALU, ACT, AX = mybir.AluOpType, mybir.ActivationFunctionType, mybir.AxisListType

P = 128
D = 2048
S = 256
T = S // P
KT = D // P
HEADS, KV, HD = 8, 2, 128
GROUP = HEADS // KV
CMP, STRIDE = 32, 16
NC = (S - CMP) // STRIDE + 1
LAT = 256
IH, ID = 4, 64
TOPK = min(256, S // 4)
GG = 8
W = 1024
NB = 3
NG, EG = 4, 4
NE = NG * EG
DE = 512
SLOTS = 64
PASSES = -(-S // SLOTS)
PAIRS = NE // 2
MRAW = 12
MU = 24
ALPHA = 2 ** 0.25
EPS = 1e-5
NEG = -1e30
TAKEN = -3e38

C_QA, C_KC, C_KS, C_KW, C_GN = 0, 1024, 1536, 2048, 2560
C_QB, C_CKV, C_QI, C_KI, C_UV, C_GM = 2584, 3608, 3864, 4120, 4188, 6236
NKI = ID + IH
NGN = HEADS * 3
NSM = NKI + NGN

UNIT = 2048
RAW, SPLIT = 6, 2
QUADS = KT // 4


class Chain:

    def __init__(self, eng, sem):
        self.eng, self.sem, self.n, self.off = eng, sem, 0, 0

    def link(self, ins):
        self.n += 1
        ins.then_inc(self.sem, 1)
        self.eng.wait_ge(self.sem, self.off + self.n)

    @contextmanager
    def loop(self, count, per):
        with self.eng.Fori(0, count) as i:
            n0, off0 = self.n, self.off
            self.off = off0 + i * per
            yield i
            assert self.n - n0 == per, (self.n - n0, per)
            self.off = off0
        self.n = n0 + per * count


def build(nc, A, out):
    offset = [1152]
    made = {}

    def at(name, off, shape, dt=F32):
        return nc.alloc_sbuf_tensor_at(name, shape, dt, offset=off)

    def sb(name, shape, dt=F32):
        size = -(-int(np.prod(shape[1:])) * 4 // 32) * 32
        off = offset[0]
        offset[0] += size
        assert offset[0] <= 229344, (name, offset[0])
        made[name] = off
        return at(name, off, shape, dt)

    with ExitStack() as ctx:
        def sem(name):
            return ctx.enter_context(nc.semaphore(name))

        raw = sb("raw", [P, RAW, UNIT])
        whi = sb("whi", [P, SPLIT, UNIT], F32R)
        wlo = sb("wlo", [P, SPLIT, UNIT], F32R)
        xhi = sb("xhi", [P, KT, S], F32R)
        xlo = sb("xlo", [P, KT, S], F32R)
        acc = sb("acc", [P, T, D])
        o1 = sb("o1", [P, 2, HEADS, S], F32R)
        o2 = sb("o2", [P, 2, HEADS, S], F32R)
        qaT = sb("qaT", [P, HEADS, S])
        qbT = sb("qbT", [P, HEADS, S])
        ksT, kwT = sb("ksT", [P, KV, S]), sb("kwT", [P, KV, S])
        vs, vw = sb("vs", [P, T, KV * HD]), sb("vw", [P, T, KV * HD])
        cT = sb("cT", [P, LAT // P, S])
        ident = sb("ident", [P, P])
        dist = sb("dist", [P, 3 * P])
        ddsa = sb("ddsa", [P, 3 * P])
        distc = sb("distc", [P, T, NC + 1])
        slopes = sb("slopes", [P, HEADS])
        rowok = sb("rowok", [P, 1])
        gall = sb("gall", [P, GROUP, 12])
        sm = sb("sm", [P, T, NSM])
        kcc = sb("kcc", [P, KV * NC + 2])
        vcc = sb("vcc", [P, KV, HD])
        qst = sb("qst", [P, 2, S])
        sP = sb("sP", [P, 4, 3 * P])
        sC = sb("sC", [P, 2, T, NC + 1])
        pT = sb("pT", [P, 4, 512])
        khT = sb("khT", [P, 2, S])
        vh = sb("vh", [P, 2, T, HD])
        wuk = sb("wuk", [P, 2, 2, HD])
        wuv = sb("wuv", [P, 2, 2, HD])
        sig = sb("sig", [P, T, 512])
        mx, rs = sb("mx", [P, 12]), sb("rs", [P, 12])
        bst, bag = sb("bst", [P, T, 4, 6]), sb("bag", [P, T, 2])
        rstd, ssq = sb("rstd", [P, T]), sb("ssq", [P, T])

        R, O1, O2 = made["acc"], made["o1"], made["o2"]
        xin = at("xin", R, [P, T, D])
        kcT, vcT = at("kcT", R, [P, KV, S]), at("vcT", R + 2048, [P, KV, S])
        XP = CMP * KV * NC
        xpk = at("xpk", R + 4096, [P, XP])
        xpkh = at("xpkh", R + 4096 + 4 * XP, [P, XP], F32R)
        xpkl = at("xpkl", R + 4096 + 8 * XP, [P, XP], F32R)
        xpv = at("xpv", O1, [P, XP])
        xpvh = at("xpvh", O1 + 4 * XP, [P, XP], F32R)
        xpvl = at("xpvl", O1 + 8 * XP, [P, XP], F32R)
        ws = at("ws", O1 + 12288, [P, GG, P])
        lng, lnb = at("lng", O1, [P, W]), at("lnb", O1 + 4096, [P, W])
        mixt = at("mixt", R, [P, GG, S])
        wsT = at("wsT", R + 8192, [P, GG, P])
        bsb = at("bsb", R + 12288, [P, GG, P])
        uT, vt = at("uT", O2, [P, GG, S]), at("vt", O2 + 8192, [P, T, W])
        w2 = at("w2", O2, [P, 2, HD])
        pein = at("pein", O2 + 1024, [2 * CMP, HD])
        peT = at("peT", O2 + 2048, [P, 2 * CMP])
        g1 = at("g1", O2 + 3072, [P, 2, 32])
        kvg = at("kvg", made["pT"], [P, LAT])
        ctm = at("ctm", made["pT"] + 1024, [P, T, LAT])
        junk = at("junk", made["pT"] + 3072, [P, LAT])
        qiT = at("qiT", made["sP"], [P, 2, S])
        kiT = at("kiT", made["sP"] + 2048, [P, S])
        kdup = at("kdup", made["sP"] + 3072, [P, T, P])
        score = at("score", made["sig"], [P, 3 * P])
        rel = at("rel", made["pT"] + 4096, [P, 2, 3 * P])
        top8 = at("top8", made["qst"], [P, T, 8])
        sgn = at("sgn", made["qst"] + 64, [P, T, NGN])

        xr = at("xr", O2, [P, T, D])
        l1g, l1b = at("l1g", made["qaT"], [P, D]), at("l1b", made["qbT"], [P, D])

        mraw = at("mraw", made["raw"], [P, MRAW, UNIT])
        assert made["xhi"] + KT * S * 4 == made["raw"] + MRAW * UNIT * 4
        xg, ysb = at("xg", made["xlo"], [P, KT, 2 * SLOTS]), at("ysb", made["xlo"] + 8192, [P, D])
        x1T = at("x1T", O1, [P, KT, S])
        l2g, l2b = at("l2g", made["qaT"], [P, D]), at("l2b", made["qbT"], [P, D])
        small = [made["ksT"], made["pT"]]

        def carve(which, name, shape, dt=F32):
            off = small[which]
            small[which] += -(-int(np.prod(shape[1:])) * 4 // 32) * 32
            return at(name, off, shape, dt)

        hh, hT = carve(0, "hh", [P, DE]), carve(0, "hT", [P, DE // P, 2 * SLOTS])
        hot, cmb = carve(0, "hot", [P, T, 2 * SLOTS]), carve(0, "cmb", [P, T, 2 * SLOTS])
        wsl = carve(0, "wsl", [P, S])
        assert small[0] <= made["ksT"] + 8192
        before, ones = carve(1, "before", [P, P]), carve(1, "ones", [P, P])
        iota64, iota4 = carve(1, "iota64", [P, SLOTS]), carve(1, "iota4", [P, NG])
        wr, br = carve(1, "wr", [P, KT, NG + NE]), carve(1, "br", [P, NG + NE])
        lg, eg = carve(1, "lg", [P, T, NG + NE]), carve(1, "eg", [P, T, NG])
        ohg, oh1, oh2, ein = (carve(1, n, [P, T, 4]) for n in ("ohg", "oh1", "oh2", "ein"))
        ein4 = carve(1, "ein4", [P, T, NG, EG])
        top1, top2, tmin, ed, gp, wt1, wt2 = (carve(1, n, [P, T]) for n in ("top1", "top2", "tmin", "ed", "gp", "wt1", "wt2"))
        sel, comb, pos = (carve(1, n, [P, T, NE]) for n in ("sel", "comb", "pos"))
        cnt, steps_i = carve(1, "cnt", [P, PASSES]), carve(1, "steps_i", [P, 1], I32)
        more_i = carve(1, "more_i", [P, 1], I32)
        assert small[1] <= made["pT"] + 8192

        main = [ctx.enter_context(nc.psum_tensor(f"main{j}", [P, 2, 512], F32)) for j in range(2)]
        att = ctx.enter_context(nc.psum_tensor("att", [P, 4, 512], F32))

        landed = [sem(f"landed{j}") for j in range(RAW)]
        hi_done, lo_done, unit_used = sem("hi_done"), sem("lo_done"), sem("unit_used")
        chunk_out = sem("chunk_out")
        step_free = sem("step_free")
        x_in, x_ps, x_hi, x_lo = sem("x_in"), sem("x_ps"), sem("x_hi"), sem("x_lo")
        gn_in, pe_in, pe_ps, pe_out, w2_in, kvg_in = (sem(n) for n in ("gn_in", "pe_in", "pe_ps", "pe_out", "w2_in", "kvg_in"))
        ws_in, ws_ps, ws_out, ws_ok = sem("ws_in"), sem("ws_ps"), sem("ws_out"), sem("ws_ok")
        late_in = sem("late_in")
        consts = sem("consts")
        pch, ach, dch = sem("pch"), sem("ach"), sem("dch")
        kd, ki_ps, ki_out, ix_ps, ix_sum, ix_mask = (sem(n) for n in ("kd", "ki_ps", "ki_out", "ix_ps", "ix_sum", "ix_mask"))
        c_ssq, c_var, c_std, c_norm, c_ps, c_out = (sem(n) for n in ("c_ssq", "c_var", "c_std", "c_norm", "c_ps", "c_out"))
        xp_sum, xp_hi, xp_lo, g1_out, cc_ps, cc_out = (sem(n) for n in ("xp_sum", "xp_hi", "xp_lo", "g1_out", "cc_ps", "cc_out"))
        gsig, v_var, v_std, v_nrm, v_ok, mix_ps, mix_u = (sem(n) for n in ("gsig", "v_var", "v_std", "v_nrm", "v_ok", "mix_ps", "mix_u"))
        oc_hi = sem("oc_hi")
        q_st, s_ps, s_max, s_exp, s_scaled, p_ps, p_out, o_ps, o_hi, att_free = (sem(n) for n in (
            "q_st", "s_ps", "s_max", "s_exp", "s_scaled", "p_ps", "p_out", "o_ps", "o_hi", "att_free"))
        uk_in = [sem(f"uk_in{j}") for j in range(4)]
        kv_ps, kh_out, vh_out = sem("kv_ps"), sem("kh_out"), sem("vh_out")
        sig_out = sem("sig_out")
        xr_in, l1_in, out_free = sem("xr_in"), sem("l1_in"), sem("out_free")
        l1_var, l1_std, l1_mul, x1_ok = sem("l1_var"), sem("l1_std"), sem("l1_mul"), sem("x1_ok")
        m_ps, m_hi, m_lo = sem("m_ps"), sem("m_hi"), sem("m_lo")
        out_done, out_ok = sem("out_done"), sem("out_ok")
        mlanded = [sem(f"mlanded{j}") for j in range(MRAW)]
        (m_used, t_ps, t_out, wr_in, br_in, r_ps, sel_ok, moe_const, pos_ps, np_ok, hot_ok, sc_free, sc_ps, xg_ps, xg_out,
         ws_t, wsl_out, h_ok, ht_ps, ht_out, y_out, silu_ok, eg_in, eg_out, ed_in, ed_out, l2_in, l2_var, l2_std) = (sem(n) for n in (
            "m_used", "t_ps", "t_out", "wr_in", "br_in", "r_ps", "sel_ok", "moe_const", "pos_ps", "np_ok", "hot_ok",
            "sc_free", "sc_ps", "xg_ps", "xg_out", "ws_t", "wsl_out", "h_ok", "ht_ps", "ht_out", "y_out", "silu_ok",
            "eg_in", "eg_out", "ed_in", "ed_out", "l2_in", "l2_var", "l2_std"))

        w_in = A["w_in"][0]
        units = []

        def chunk_units(c0):
            for q in range(QUADS):
                src = w_in[q * 512:(q + 1) * 512, c0:c0 + 512].rearrange("(k p) n -> p k n", p=P)
                units.append((src, 4, 512))

        units.append((w_in[:, C_KI:C_KI + NKI].rearrange("(k p) n -> p k n", p=P), KT, NSM))
        chunks = {"small": (0, 0)}

        def chunk(name, c0):
            chunks[name] = (len(chunks), len(units))
            chunk_units(c0)

        chunk("ckv", C_CKV)
        chunk("kcvc", C_KC)
        chunk("slc", C_KS)
        w1u = len(units)
        for j in range(2):
            for q in range(2):
                src = A["cmp_w1"][0, j, q * 2048:(q + 1) * 2048, :].rearrange("(l p) m -> p l m", p=P)
                units.append((src, 16, P))
        chunk("win", C_KW)
        chunk("qa0", C_QA)
        chunk("qa1", C_QA + 512)
        chunk("v0", C_UV + W)
        chunk("v1", C_UV + W + 512)
        chunk("qb0", C_QB)
        chunk("qb1", C_QB + 512)
        chunk("u0", C_UV)
        chunk("u1", C_UV + 512)
        U0 = len(units)
        NCH = len(chunks)
        UB = QUADS + 2
        BR = [2, 0, 1]
        U1 = U0 + NB * 4 * UB
        assert UB % RAW == 0 and UB % SPLIT == 0

        def last(name):
            return chunks[name][1] + QUADS - 1

        def view(tensor, slot, k, n):
            return tensor[:, slot, 0:k * n].rearrange("p (k n) -> p k n", n=n)

        def expert_unit(r, pair):
            e = pair * 2 + r % 2
            if r < 4 * QUADS:
                q, name = r // 4, ("expert_w_gate", "expert_w_up")[r % 4 // 2]
                rows = A[name][0, bass.ds(e, 1), q * 512:(q + 1) * 512, :]
                return rows.rearrange("a (k p) f -> p (a k) f", p=P)
            kf = (r - 4 * QUADS) // 2
            return A["expert_w_down"][0, bass.ds(e, 1), kf * P:(kf + 1) * P, :].rearrange("a p d -> p a d")

        def moe_loads(sp):
            def load(r, pair, turn):
                slot = r % MRAW
                if turn is not None:
                    sp.wait_ge(m_used, turn)
                dst = mraw[:, slot, :]
                if r < 4 * QUADS:
                    dst = dst.rearrange("p (k f) -> p k f", f=DE)
                else:
                    dst = dst.unsqueeze(1)
                sp.dma_start(dst, expert_unit(r, pair)).then_inc(mlanded[slot], 16)

            sp.wait_ge(lo_done, U1 + 4 * QUADS)
            for r in range(MRAW):
                if r == RAW:
                    sp.wait_ge(unit_used, U1 + 4 * QUADS)
                load(r, 0, None)
            sp.wait_ge(np_ok, 1)
            more = sp.value_load(more_i[0:1, 0:1], min_val=PAIRS - 1, max_val=PAIRS * PASSES - 1)
            with sp.Fori(0, more) as m:
                for r in range(MRAW, MU):
                    load(r, (m + (0 if r < 4 * QUADS else PAIRS)) % PAIRS, m * MU + r - MRAW + 1)
                for r in range(MRAW):
                    load(r, (m + 1) % PAIRS, m * MU + MU + r - MRAW + 1)
            for r in range(MRAW, MU):
                load(r, PAIRS - 1, more * MU + r - MRAW + 1)

        def moe_pe(pe):
            for j in range(KT // 2):
                if j == 0:
                    pe.wait_ge(x1_ok, T)
                if j >= 4:
                    pe.wait_ge(t_out, j - 3)
                for kk in range(2):
                    for t in range(T):
                        k = 2 * j + kk
                        ins = pe.transpose(att[:, j % 4, (kk * T + t) * P:(kk * T + t + 1) * P],
                                           xr[:, t, k * P:(k + 1) * P], ident[:])
                ins.then_inc(t_ps, 1)
            pe.wait_ge(wr_in, 32)
            pe.wait_ge(out_free, 4)
            for t in range(T):
                for k in range(KT):
                    if t == 0 and k % 2 == 0:
                        pe.wait_ge(t_out, k // 2 + 1)
                    ins = pe.matmul(main[0][:, 0, t * 32:t * 32 + NG + NE], x1T[:, k, t * P:(t + 1) * P], wr[:, k, :],
                                    start=(k == 0 and t == 0), stop=(k == KT - 1), skip_group_check=True)
            ins.then_inc(r_ps, 1)
            pe.wait_ge(sel_ok, 1)
            pe.wait_ge(moe_const, 2)
            r_ = main[1][:, 0, :]
            pe.matmul(r_[:, 0:NE], before[:], sel[:, 0, :], start=True, stop=True, skip_group_check=True)
            pe.matmul(r_[:, NE:2 * NE], ones[:], sel[:, 0, :], start=False, stop=False, skip_group_check=True)
            pe.matmul(r_[:, NE:2 * NE], before[:], sel[:, 1, :], start=False, stop=True, skip_group_check=True)
            pe.matmul(r_[:, 2 * NE:3 * NE], ones[:], sel[:, 0, :], start=False, stop=False, skip_group_check=True)
            pe.matmul(r_[:, 2 * NE:3 * NE], ones[:], sel[:, 1, :], start=False, stop=True, skip_group_check=True).then_inc(pos_ps, 1)
            pe.wait_ge(np_ok, 1)
            steps = pe.value_load(steps_i[0:1, 0:1], min_val=PAIRS, max_val=PAIRS * PASSES)
            with pe.Fori(0, steps) as m:
                pe.wait_ge(hot_ok, 1 + m)
                pe.wait_ge(sc_free, 1 + m * 8)
                for k in range(KT):
                    for t in range(T):
                        ins = pe.matmul(att[:, k // 4, k % 4 * P:(k % 4 + 1) * P], xr[:, t, k * P:(k + 1) * P], hot[:, t, :],
                                        start=(k % 4 == 0 and t == 0), stop=(t == 1), skip_group_check=True)
                    if k % 4 == 3:
                        ins.then_inc(xg_ps, 1)
                for t in range(T):
                    ins = pe.transpose(main[1][:, 1, t * P:(t + 1) * P], cmb[:, t, :], ident[:])
                ins.then_inc(ws_t, 1)
                for q in range(QUADS):
                    pe.wait_ge(xg_out, 1 + q + m * 4)
                    for s_ in range(4):
                        r = 4 * q + s_
                        pe.wait_ge(mlanded[r % MRAW], 16 * (r // MRAW + 1) + m * 32)
                    for kk in range(4):
                        k = 4 * q + kk
                        for s_ in range(4):
                            a, w = s_ % 2, mraw[:, (4 * q + s_) % MRAW, kk * DE:(kk + 1) * DE]
                            half = slice(a * SLOTS, (a + 1) * SLOTS)
                            ins = pe.matmul(main[0][half, s_ // 2, :], xg[:, k, half], w, start=(k == 0),
                                            stop=(k == KT - 1))
                            if kk == 3:
                                ins.then_inc(m_used, 1)
                pe.wait_ge(h_ok, 1 + m)
                for f in range(DE // P):
                    ins = pe.transpose(main[1][:, 0, f * P:(f + 1) * P], hh[:, f * P:(f + 1) * P], ident[:])
                ins.then_inc(ht_ps, 1)
                pe.wait_ge(ht_out, 1 + m)
                for f in range(DE // P):
                    for a in range(2):
                        r = 4 * QUADS + 2 * f + a
                        pe.wait_ge(mlanded[r % MRAW], 16 * (r // MRAW + 1) + m * 32)
                    for c in range(4):
                        for a in range(2):
                            r = 4 * QUADS + 2 * f + a
                            half = slice(a * SLOTS, (a + 1) * SLOTS)
                            ins = pe.matmul(att[half, c, :], hT[:, f, half], mraw[:, r % MRAW, c * 512:(c + 1) * 512],
                                            start=(f == 0), stop=(f == DE // P - 1))
                            if c == 3:
                                ins.then_inc(m_used, 1)
                pe.wait_ge(wsl_out, 1 + m)
                for c in range(4):
                    pe.wait_ge(y_out, 1 + c + m * 4)
                    for t in range(T):
                        n = c * T + t
                        if n >= 2:
                            pe.wait_ge(sc_free, n + m * 8)
                        pe.matmul(main[1][:, t, :], wsl[:, t * P:(t + 1) * P], ysb[:, c * 512:(c + 1) * 512],
                                  start=True, stop=True).then_inc(sc_ps, 1)

        def act_tail(act):
            for t in range(T):
                act.wait_ge(l1_var, t + 1)
                act.activation(rstd[:, t:t + 1], bag[:, t, 1:2], ACT.Sqrt).then_inc(l1_std, 1)
            act.dma_start(wr[:, :, 0:NG], A["router_group_w"][0].rearrange("(k p) n -> p k n", p=P)).then_inc(wr_in, 16)
            act.dma_start(wr[:, :, NG:NG + NE], A["router_expert_w"][0].rearrange("(k p) n -> p k n", p=P)).then_inc(wr_in, 16)
            act.dma_start(br[:, 0:NG], A["router_group_b"].to_broadcast([P, NG])).then_inc(br_in, 16)
            act.dma_start(br[:, NG:NG + NE], A["router_expert_b"].to_broadcast([P, NE])).then_inc(br_in, 16)
            for j in range(KT // 2):
                act.wait_ge(t_ps, j + 1)
                act.activation(x1T[:, 2 * j:2 * j + 2, :].rearrange("p k s -> p (k s)"), att[:, j % 4, :],
                               ACT.Copy).then_inc(t_out, 1)
            act.wait_ge(x1_ok, T)
            act.dma_start(l2g[:], A["ln2_g"].to_broadcast([P, D])).then_inc(l2_in, 16)
            act.dma_start(l2b[:], A["ln2_b"].to_broadcast([P, D])).then_inc(l2_in, 16)
            act.wait_ge(eg_in, 1)
            act.activation(eg[:], lg[:, :, 0:NG], ACT.Exp).then_inc(eg_out, 1)
            act.wait_ge(ed_in, 1)
            act.activation(ed[:], ed[:], ACT.Exp).then_inc(ed_out, 1)
            act.wait_ge(np_ok, 1)
            steps = act.value_load(steps_i[0:1, 0:1], min_val=PAIRS, max_val=PAIRS * PASSES)
            with act.Fori(0, steps) as m:
                for q in range(4):
                    act.wait_ge(xg_ps, 1 + q + m * 4)
                    act.activation(xg[:, 4 * q:4 * q + 4, :].rearrange("p k s -> p (k s)"), att[:, q, :],
                                   ACT.Copy).then_inc(xg_out, 1)
                act.wait_ge(ws_t, 1 + m)
                act.activation(wsl[:], main[1][:, 1, 0:S], ACT.Copy).then_inc(wsl_out, 1)
                act.wait_ge(m_used, 4 * QUADS + m * MU)
                act.activation(hh[:], main[0][:, 0, :], ACT.Silu).then_inc(silu_ok, 1)
                act.wait_ge(ht_ps, 1 + m)
                act.activation(hT[:].rearrange("p f s -> p (f s)"), main[1][:, 0, :], ACT.Copy).then_inc(ht_out, 1)
                act.wait_ge(m_used, MU + m * MU)
                for c in range(4):
                    act.activation(ysb[:, c * 512:(c + 1) * 512], att[:, c, :], ACT.Copy).then_inc(y_out, 1)
            for t in range(T):
                act.wait_ge(l2_var, t + 1)
                act.activation(rstd[:, t:t + 1], bag[:, t, 1:2], ACT.Sqrt).then_inc(l2_std, 1)

        def dve_moe(dve, ch):
            link = ch.link
            dve.wait_ge(br_in, 32)
            dve.wait_ge(r_ps, 1)
            dve.wait_ge(moe_const, 3)
            psl = main[0][:, 0, 0:64].rearrange("p (t n) -> p t n", t=T)[:, :, 0:NG + NE]
            link(dve.tensor_tensor(lg[:], psl, br[:].unsqueeze(1).to_broadcast([P, T, NG + NE]), ALU.add))
            io4 = iota4[:].unsqueeze(1).to_broadcast([P, T, NG])

            def first_max(dst, x, top):
                link(dve.tensor_reduce(top, x, AX.X, ALU.max))
                link(dve.tensor_tensor(dst, x, top.unsqueeze(2).to_broadcast([P, T, 4]), ALU.is_equal))
                link(dve.tensor_tensor(dst, dst, io4, ALU.mult))
                link(dve.tensor_reduce(tmin[:], dst, AX.X, ALU.min))
                link(dve.tensor_tensor(dst, io4, tmin[:].unsqueeze(2).to_broadcast([P, T, 4]), ALU.is_equal))

            first_max(ohg[:], lg[:, :, 0:NG], top1[:])
            dve.tensor_tensor(lg[:, :, 0:NG], lg[:, :, 0:NG], top1[:].unsqueeze(2).to_broadcast([P, T, NG]),
                              ALU.subtract).then_inc(eg_in, 1)
            ev = lg[:, :, NG:NG + NE].rearrange("p t (g e) -> p t g e", g=NG)
            ohb = ohg[:].unsqueeze(3).to_broadcast([P, T, NG, EG])
            for t in range(T):
                ins = dve.tensor_tensor(ein4[:, t], ev[:, t], ohb[:, t], ALU.mult)
            link(ins)
            for t in range(T):
                ins = dve.tensor_reduce(ein[:, t, :], ein4[:, t].rearrange("p g e -> p e g"), AX.X, ALU.add)
            link(ins)
            first_max(oh1[:], ein[:], top1[:])
            link(dve.scalar_tensor_tensor(ein[:], oh1[:], NEG, ein[:], ALU.mult, ALU.add))
            first_max(oh2[:], ein[:], top2[:])
            dve.tensor_tensor(ed[:], top2[:], top1[:], ALU.subtract).then_inc(ed_in, 1)
            link(dve.tensor_tensor(ein[:], oh1[:], oh2[:], ALU.add))
            for t in range(T):
                ins = dve.tensor_tensor(sel[:, t, :].rearrange("p (g e) -> p g e", g=NG), ohb[:, t],
                                        ein[:, t, :].unsqueeze(1).to_broadcast([P, NG, EG]), ALU.mult)
            ins.then_inc(sel_ok, 1)
            dve.wait_ge(eg_out, 1)
            link(dve.tensor_reduce(gp[:], eg[:], AX.X, ALU.add))
            link(dve.reciprocal(gp[:], gp[:]))
            dve.wait_ge(ed_out, 1)
            link(dve.tensor_scalar(wt1[:], ed[:], 1.0, None, ALU.add))
            link(dve.reciprocal(wt1[:], wt1[:]))
            link(dve.tensor_tensor(wt1[:], wt1[:], gp[:], ALU.mult))
            link(dve.tensor_tensor(wt2[:], wt1[:], ed[:], ALU.mult))
            for oh, wt in ((oh1, wt1), (oh2, wt2)):
                ins = dve.tensor_tensor(oh[:], oh[:], wt[:].unsqueeze(2).to_broadcast([P, T, 4]), ALU.mult)
            link(ins)
            link(dve.tensor_tensor(ein[:], oh1[:], oh2[:], ALU.add))
            for t in range(T):
                ins = dve.tensor_tensor(comb[:, t, :].rearrange("p (g e) -> p g e", g=NG), ohb[:, t],
                                        ein[:, t, :].unsqueeze(1).to_broadcast([P, NG, EG]), ALU.mult)
            link(ins)
            dve.wait_ge(pos_ps, 1)
            r_ = main[1][:, 0, :]
            dve.tensor_copy(pos[:].rearrange("p t e -> p (t e)"), r_[:, 0:2 * NE])
            link(dve.tensor_reduce(cnt[:, 0:1], r_[:, 2 * NE:3 * NE], AX.X, ALU.max))
            for c in range(1, PASSES):
                ins = dve.tensor_scalar(cnt[:, c:c + 1], cnt[:, 0:1], float(c * SLOTS), float(PAIRS), ALU.is_gt, ALU.mult)
            link(ins)
            link(dve.tensor_reduce(cnt[:, 0:1], cnt[:, 1:PASSES], AX.X, ALU.add))
            dve.tensor_scalar(more_i[:], cnt[:, 0:1], float(PAIRS - 1), None, ALU.add)
            dve.tensor_scalar(steps_i[:], cnt[:, 0:1], float(PAIRS), None, ALU.add).then_inc(np_ok, 1)
            for t in range(T):
                ins = dve.tensor_scalar(acc[:, t, :], xr[:, t, :], ALPHA, None, ALU.mult)
            ins.then_inc(sc_free, 1)
            dve.wait_ge(np_ok, 1)
            steps = dve.value_load(steps_i[0:1, 0:1], min_val=PAIRS, max_val=PAIRS * PASSES)
            with dve.Fori(0, steps) as m:
                pair = m % PAIRS
                dve.wait_ge(sc_free, 1 + m * 8)
                for t in range(T):
                    for a in range(2):
                        e = bass.ds(pair * 2 + a, 1)
                        half = slice(a * SLOTS, (a + 1) * SLOTS)
                        dve.tensor_scalar(hot[:, t, half], iota64[:], pos[:, t, e], sel[:, t, e], ALU.is_equal, ALU.mult)
                        ins = dve.tensor_scalar(cmb[:, t, half], iota64[:], pos[:, t, e], comb[:, t, e], ALU.is_equal, ALU.mult)
                ins.then_inc(hot_ok, 1)
                dve.wait_ge(hot_ok, 1 + m)
                pe_ = pos[:, :, bass.ds(pair * 2, 2)]
                dve.tensor_scalar(pe_, pe_, float(-SLOTS), None, ALU.add)
                dve.wait_ge(silu_ok, 1 + m)
                dve.tensor_tensor(hh[:], hh[:], main[0][:, 1, :], ALU.mult).then_inc(h_ok, 1)
                for n in range(4 * T):
                    c, t = n // T, n % T
                    dve.wait_ge(sc_ps, n + 1 + m * 8)
                    a_ = acc[:, t, c * 512:(c + 1) * 512]
                    dve.tensor_tensor(a_, a_, main[1][:, t, :], ALU.add).then_inc(sc_free, 1)
            dve.wait_ge(sc_free, 1 + steps * 8)
            for t in range(T):
                for c in range(4):
                    ins = dve.bn_stats(bst[:, t, c, :], acc[:, t, c * 512:(c + 1) * 512])
                link(ins)
                link(dve.bn_aggr(bag[:, t, :], bst[:, t].rearrange("p a b -> p (a b)")))
                dve.tensor_scalar(bag[:, t, 1:2], bag[:, t, 1:2], EPS, None, ALU.add).then_inc(l2_var, 1)
            dve.wait_ge(l2_in, 32)
            for t in range(T):
                dve.wait_ge(l2_std, t + 1)
                link(dve.reciprocal(rstd[:, t:t + 1], rstd[:, t:t + 1]))
                link(dve.tensor_scalar(acc[:, t, :], acc[:, t, :], bag[:, t, 0:1], rstd[:, t:t + 1], ALU.subtract, ALU.mult))
                link(dve.tensor_tensor(acc[:, t, :], acc[:, t, :], l2g[:], ALU.mult))
                dve.tensor_tensor(acc[:, t, :], acc[:, t, :], l2b[:], ALU.add).then_inc(out_ok, 1)

        def dve_tail(dve, link, lo_at):
            def residual(c):
                if c == 0:
                    dve.wait_ge(xr_in, 16)
                dve.wait_ge(unit_used, U1 + (c + 1) * QUADS)
                cols = slice(c * 512, (c + 1) * 512)
                for t in range(T):
                    ins = dve.scalar_tensor_tensor(xr[:, t, cols], xr[:, t, cols], ALPHA, main[c % 2][:, t, :],
                                                   ALU.mult, ALU.add)
                ins.then_inc(out_free, 1)
                dve.wait_ge(out_free, c + 1)
                for t in range(T):
                    ins = dve.bn_stats(bst[:, t, c, :], xr[:, t, cols])
                return ins

            for u in range(U1 + 2, U1 + 16):
                lo_at(u)
                if (u - U1 - 2) % QUADS == QUADS - 1:
                    residual((u - U1 - 2) // QUADS)
            ins = residual(3)
            link(ins)
            for t in range(T):
                link(dve.bn_aggr(bag[:, t, :], bst[:, t].rearrange("p a b -> p (a b)")))
                dve.tensor_scalar(bag[:, t, 1:2], bag[:, t, 1:2], EPS, None, ALU.add).then_inc(l1_var, 1)
            dve.wait_ge(l1_in, 32)
            for t in range(T):
                dve.wait_ge(l1_std, t + 1)
                link(dve.reciprocal(rstd[:, t:t + 1], rstd[:, t:t + 1]))
                link(dve.tensor_scalar(xr[:, t, :], xr[:, t, :], bag[:, t, 0:1], rstd[:, t:t + 1], ALU.subtract, ALU.mult))
                link(dve.tensor_tensor(xr[:, t, :], xr[:, t, :], l1g[:], ALU.mult))
                dve.tensor_tensor(xr[:, t, :], xr[:, t, :], l1b[:], ALU.add).then_inc(x1_ok, 1)

        block = ctx.enter_context(nc.Block())

        @block.sync
        def _(sp):
            for t in range(T):
                sp.dma_start(xin[:, t, :], A["x"][0, t * P:(t + 1) * P, :]).then_inc(x_in, 16)

            def load(u, slot, src, k, n, turn=None):
                if turn is None:
                    if u >= RAW:
                        sp.wait_ge(lo_done, u - RAW + 1)
                else:
                    sp.wait_ge(lo_done, turn)
                width = src.shape[-1]
                sp.dma_start(view(raw, slot, k, n)[:, :, 0:width], src).then_inc(landed[slot], 16)

            for u, (src, k, n) in enumerate(units):
                load(u, u % RAW, src, k, n)
                if u == 0:
                    sp.dma_start(view(raw, 0, KT, NSM)[:, :, NKI:NSM],
                                 w_in[:, C_GN:C_GN + NGN].rearrange("(k p) n -> p k n", p=P)).then_inc(gn_in, 16)
            for b, n in enumerate(BR):
                with sp.Fori(0, 4) as i:
                    for j in range(UB):
                        u = U0 + b * 4 * UB + j
                        if j < QUADS:
                            src = w_in[j * 512:(j + 1) * 512, bass.ds(C_GM + n * D + i * 512, 512)]
                        else:
                            q = j - QUADS
                            col = (i + 4) % 4 * 512
                            src = A["w_branch"][0, n, q * 512:(q + 1) * 512, bass.ds(col, 512)]
                        load(u, u % RAW, src.rearrange("(k p) n -> p k n", p=P), 4, 512,
                             turn=u - RAW + 1 + i * UB)
            sp.wait_ge(unit_used, U0 + 8 * UB)
            sp.wait_ge(q_st, 8)
            sp.dma_start(xr[:], A["x"][0].rearrange("(t p) d -> p t d", p=P)).then_inc(xr_in, 16)
            sp.dma_start(l1g[:], A["ln1_g"].to_broadcast([P, D])).then_inc(l1_in, 16)
            sp.dma_start(l1b[:], A["ln1_b"].to_broadcast([P, D])).then_inc(l1_in, 16)
            for c in range(4):
                for q in range(QUADS):
                    u = U1 + c * QUADS + q
                    src = A["w_out"][0, q * 512:(q + 1) * 512, c * 512:(c + 1) * 512]
                    load(u, u % RAW, src.rearrange("(k p) n -> p k n", p=P), 4, 512)
            moe_loads(sp)
            for t in range(T):
                sp.wait_ge(out_ok, t + 1)
                sp.dma_start(out[0, t * P:(t + 1) * P, :], acc[:, t, :]).then_inc(out_done, 16)
            sp.wait_ge(out_done, 16 * T)

        @block.gpsimd
        def _(pool):
            ch = Chain(pool, pch)
            ch.link(pool.memset(ident[:], 0.0))
            pool.affine_select(out=ident[:], in_=ident[:], compare_op=ALU.not_equal, fill=1.0, base=0,
                               pattern=[[-1, P]], channel_multiplier=1).then_inc(consts, 1)
            for q in range(T):
                seg = dist[:, q * P:(1 + 2 * q) * P] if q else dist[:, 0:P]
                n = (q + 1) * P
                ch.link(pool.iota(seg, pattern=[[1, n]], base=-q * P, channel_multiplier=-1,
                                  allow_small_or_imprecise_dtypes=True))
                pool.affine_select(out=seg, in_=seg, compare_op=ALU.is_ge, fill=NEG, base=q * P,
                                   pattern=[[-1, n]], channel_multiplier=1).then_inc(consts, 1)
                ch.link(pool.iota(distc[:, q, 0:NC], pattern=[[STRIDE, NC]], base=CMP - 1 - q * P,
                                  channel_multiplier=-1, allow_small_or_imprecise_dtypes=True))
                pool.affine_select(out=distc[:, q, 0:NC], in_=distc[:, q, 0:NC], compare_op=ALU.is_ge, fill=NEG,
                                   base=q * P - CMP + 1, pattern=[[-STRIDE, NC]], channel_multiplier=1).then_inc(consts, 1)
            for h in range(HEADS):
                pool.memset(slopes[:, h:h + 1], 2.0 ** (-8.0 * (h + 1) / HEADS)).then_inc(consts, 1)
            ch.link(pool.memset(rowok[:], 1.0))
            pool.affine_select(out=rowok[:], in_=rowok[:], compare_op=ALU.is_ge, fill=0.0, base=1 - CMP,
                               pattern=[[0, 1]], channel_multiplier=1).then_inc(consts, 1)
            pool.wait_ge(ix_sum, 1)
            for q in range(T):
                seg = score[:, q * P:(1 + 2 * q) * P] if q else score[:, 0:P]
                pool.affine_select(out=seg, in_=seg, compare_op=ALU.is_ge, fill=NEG, base=q * P,
                                   pattern=[[-1, (q + 1) * P]], channel_multiplier=1).then_inc(ix_mask, 1)
            pool.wait_ge(ws_out, 2)
            pool.affine_select(out=wsT[:], in_=wsT[:], compare_op=ALU.is_ge, fill=0.0, base=0,
                               pattern=[[0, GG], [1, P]], channel_multiplier=-1).then_inc(ws_ok, 1)
            pool.wait_ge(late_in, 48)
            for t in range(T):
                pool.wait_ge(v_nrm, t + 1)
                ch.link(pool.tensor_tensor(vt[:, t, :], vt[:, t, :], lng[:], ALU.mult))
                pool.tensor_tensor(vt[:, t, :], vt[:, t, :], lnb[:], ALU.add).then_inc(v_ok, 1)
            pool.wait_ge(l1_var, 1)
            ch.link(pool.memset(before[:], 1.0))
            pool.affine_select(out=before[:], in_=before[:], compare_op=ALU.is_ge, fill=0.0, base=-1,
                               pattern=[[1, P]], channel_multiplier=-1).then_inc(moe_const, 1)
            pool.memset(ones[:], 1.0).then_inc(moe_const, 1)
            pool.iota(iota4[:], pattern=[[1, NG]], base=-8, channel_multiplier=0, allow_small_or_imprecise_dtypes=True)
            pool.iota(iota64[:], pattern=[[1, SLOTS]], base=0, channel_multiplier=0,
                      allow_small_or_imprecise_dtypes=True).then_inc(moe_const, 1)
        N_CONST = 1 + 2 * T + HEADS + 1

        @block.tensor
        def _(pe):
            pe.wait_ge(consts, 1)
            pe.wait_ge(pe_in, 16)
            pe.transpose(att[:, 0, 0:2 * CMP], pein[:], ident[0:2 * CMP, 0:2 * CMP]).then_inc(pe_ps, 1)
            pe.wait_ge(x_in, 16 * T)
            for j in range(KT // 2):
                if j >= 4:
                    pe.wait_ge(x_lo, j - 3)
                bank = main[j % 4 // 2][:, j % 2, :]
                for kk in range(2):
                    for t in range(T):
                        k = 2 * j + kk
                        ins = pe.transpose(bank[:, (kk * T + t) * P:(kk * T + t + 1) * P],
                                           xin[:, t, k * P:(k + 1) * P], ident[:])
                ins.then_inc(x_ps, 1)
            pe.wait_ge(x_lo, KT // 2)

            def mm3(o, ah, al, bh, bl, start, stop, skip=False):
                pe.matmul(o, ah, bh, start=start, stop=False, skip_group_check=skip)
                pe.matmul(o, ah, bl, start=False, stop=False, skip_group_check=skip)
                return pe.matmul(o, al, bh, start=False, stop=stop, skip_group_check=skip)

            def tokens(o, k, t, bh, bl, start, stop, skip=False):
                cols = slice(t * P, (t + 1) * P)
                return mm3(o, xhi[:, k, cols], xlo[:, k, cols], bh, bl, start, stop, skip)

            def features(o, k, wh, wl, start, stop, skip=False):
                return mm3(o, wh, wl, xhi[:, k, :], xlo[:, k, :], start, stop, skip)

            def unit_ready(u):
                pe.wait_ge(lo_done, u + 1)

            def start_chunk(name):
                c = chunks[name][0]
                if c >= 2:
                    pe.wait_ge(chunk_out, c - 1)
                return main[c % 2], chunks[name][1]

            def feature_chunk(name, hook=None):
                ps, u0 = start_chunk(name)
                for q in range(QUADS):
                    u = u0 + q
                    unit_ready(u)
                    wh, wl = view(whi, u % SPLIT, 4, 512), view(wlo, u % SPLIT, 4, 512)
                    for kk in range(4):
                        for m in range(4):
                            k = 4 * q + kk
                            ins = features(ps[:, m // 2, m % 2 * S:(m % 2 + 1) * S], k,
                                           wh[:, kk, m * P:(m + 1) * P], wl[:, kk, m * P:(m + 1) * P],
                                           k == 0 and m % 2 == 0, k == KT - 1, True)
                    ins.then_inc(unit_used, 1)
                    if hook:
                        hook(u)

            def mixed_chunk(name, f0, t0, hook=None):
                ps, u0 = start_chunk(name)
                for q in range(QUADS):
                    u = u0 + q
                    unit_ready(u)
                    wh, wl = view(whi, u % SPLIT, 4, 512), view(wlo, u % SPLIT, 4, 512)
                    for kk in range(4):
                        k = 4 * q + kk
                        for m in range(2):
                            c = f0 + m * P
                            features(ps[:, 0, m * S:(m + 1) * S], k, wh[:, kk, c:c + P], wl[:, kk, c:c + P],
                                     k == 0 and m == 0, k == KT - 1, True)
                        for t in range(T):
                            ins = tokens(ps[:, 1, t * 256:(t + 1) * 256], k, t, wh[:, kk, t0:t0 + 256],
                                         wl[:, kk, t0:t0 + 256], k == 0 and t == 0, k == KT - 1, True)
                    ins.then_inc(unit_used, 1)
                    if hook:
                        hook(u)

            def token_chunk(name, hook=None):
                ps, u0 = start_chunk(name)
                for q in range(QUADS):
                    u = u0 + q
                    unit_ready(u)
                    wh, wl = view(whi, u % SPLIT, 4, 512), view(wlo, u % SPLIT, 4, 512)
                    for kk in range(4):
                        k = 4 * q + kk
                        for t in range(T):
                            ins = tokens(ps[:, t, :], k, t, wh[:, kk, :], wl[:, kk, :], k == 0, k == KT - 1)
                    ins.then_inc(unit_used, 1)
                    if hook:
                        hook(u)

            unit_ready(0)
            wh, wl = view(whi, 0, KT, NSM), view(wlo, 0, KT, NSM)
            for k in range(KT):
                for t in range(T):
                    ins = tokens(main[0][:, 0, t * NSM:(t + 1) * NSM], k, t, wh[:, k, :], wl[:, k, :],
                                 k == 0 and t == 0, k == KT - 1, True)
            ins.then_inc(unit_used, 1)

            def index_key(u):
                if u == last("ckv"):
                    pe.wait_ge(kd, 1)
                    pe.wait_ge(pe_out, 1)
                    for t in range(T):
                        ins = pe.transpose(att[:, 0, t * P:(t + 1) * P], kdup[:, t, :], ident[:])
                    ins.then_inc(ki_ps, 1)

            mixed_chunk("ckv", 256, 0, index_key)

            def index_scores(u):
                if u == chunks["kcvc"][1] + 2:
                    pe.wait_ge(ki_out, 1)
                    pe.wait_ge(chunk_out, 2)
                    for h in range(IH):
                        rows = slice(h % 2 * ID, h % 2 * ID + ID)
                        for q in range(T):
                            ins = pe.matmul(att[:, h, q * P:(1 + 2 * q) * P if q else P],
                                            qiT[rows, h // 2, q * P:(q + 1) * P], kiT[rows, 0:(q + 1) * P],
                                            start=(q == 0), stop=True, skip_group_check=True)
                    ins.then_inc(ix_ps, 1)

            feature_chunk("kcvc", index_scores)

            def latent_T(u):
                if u == last("slc"):
                    pe.wait_ge(c_norm, T)
                    pe.wait_ge(ix_sum, 1)
                    for c in range(LAT // P):
                        for t in range(T):
                            ins = pe.transpose(att[:, 2, (c * T + t) * P:(c * T + t + 1) * P],
                                               ctm[:, t, c * P:(c + 1) * P], ident[:])
                    ins.then_inc(c_ps, 1)

            mixed_chunk("slc", 0, 256, latent_T)

            for j, (xh, xl) in enumerate(((xpkh, xpkl), (xpvh, xpvl))):
                pe.wait_ge(xp_lo, j + 1)
                for q in range(2):
                    u = w1u + 2 * j + q
                    unit_ready(u)
                    wh, wl = view(whi, u % SPLIT, 16, P), view(wlo, u % SPLIT, 16, P)
                    for l in range(16):
                        cols = slice((q * 16 + l) * KV * NC, (q * 16 + l + 1) * KV * NC)
                        first = q == 0 and l == 0
                        ins = mm3(att[:, 3, j * 32:j * 32 + KV * NC], wh[:, l, :], wl[:, l, :], xh[:, cols],
                                  xl[:, cols], first and j == 0, q == 1 and l == 15, True)
                    ins.then_inc(unit_used, 1)

            def compress2(u):
                if u == chunks["win"][1] + 1:
                    pe.wait_ge(g1_out, 1)
                    pe.wait_ge(w2_in, 16)
                    pe.matmul(att[:, 3, 0:KV * NC], w2[:, 0, :], g1[:, 0, 0:KV * NC], start=True, stop=True)
                    for h in range(KV):
                        ins = pe.matmul(att[0:NC, 3, 256 + h * HD:256 + (h + 1) * HD],
                                        g1[:, 1, h * NC:(h + 1) * NC], w2[:, 1, :], start=True, stop=True)
                    ins.then_inc(cc_ps, 1)
                if u == last("win"):
                    pe.wait_ge(ws_in, 16)
                    for g in range(GG):
                        ins = pe.transpose(att[:, g // 4, g % 4 * P:(g % 4 + 1) * P], ws[:, g, :], ident[:])
                        if g % 4 == 3:
                            ins.then_inc(ws_ps, 1)

            mixed_chunk("win", 0, 256, compress2)
            feature_chunk("qa0")
            feature_chunk("qa1")
            token_chunk("v0")
            token_chunk("v1")
            feature_chunk("qb0")

            def spatial(u):
                if u == last("qb1"):
                    pe.wait_ge(v_ok, T)
                    pe.wait_ge(ws_ok, 1)
                    pe.wait_ge(c_out, 1)
                    pe.wait_ge(cc_out, 2)
                    for g in range(GG):
                        for c in range(T):
                            ins = pe.matmul(att[:, g // 2, (g % 2 * T + c) * P:(g % 2 * T + c + 1) * P],
                                            vt[:, c, g * HD:(g + 1) * HD], wsT[:, g, :], start=True, stop=True,
                                            skip_group_check=True)
                    ins.then_inc(mix_ps, 1)

            feature_chunk("qb1", spatial)
            feature_chunk("u0")
            feature_chunk("u1")

            def scores(n_done, nsa):
                pe.wait_ge(q_st, n_done)
                for a in range(2):
                    for s_, kT in enumerate((ksT, kwT) if nsa else (khT,)):
                        bank = att[:, 2 * a + s_, :] if nsa else att[:, a, :]
                        for q in range(T):
                            ins = pe.matmul(bank[:, P:3 * P] if q else bank[:, 0:P], qst[:, a, q * P:(q + 1) * P],
                                            kT[:, a, 0:(q + 1) * P], start=(q == 0), stop=True,
                                            skip_group_check=True)
                            if nsa and s_ == 1:
                                ins = pe.matmul(att[:, 2 * a, 3 * P + q * 16:3 * P + q * 16 + NC],
                                                qst[:, a, q * P:(q + 1) * P], kcc[:, a * NC:(a + 1) * NC],
                                                start=False, stop=True, skip_group_check=True)
                ins.then_inc(s_ps, 1)

            def transposes(n_done, nsa):
                pe.wait_ge(s_scaled, n_done)
                for a in range(2):
                    for s_ in range(2 if nsa else 1):
                        seg = 2 * a + s_ if nsa else a
                        for blk in range(3):
                            ins = pe.transpose(att[:, seg, blk * P:(blk + 1) * P], sP[:, seg, blk * P:(blk + 1) * P], ident[:])
                        if nsa:
                            ins = pe.transpose(att[0:NC, seg, 3 * P:4 * P], sC[:, a, s_, 0:NC], ident[:])
                ins.then_inc(p_ps, 1)

            def values(n_done, nsa):
                pe.wait_ge(p_out, n_done)
                for a in range(2):
                    o = att[:, a, 0:S]
                    for s_ in range(2 if nsa else 1):
                        seg = 2 * a + s_ if nsa else a
                        for st in range(T):
                            if nsa:
                                v = (vs, vw)[s_][:, st, a * HD:(a + 1) * HD]
                            else:
                                v = vh[:, a, st, :]
                            ins = pe.matmul(o if st == 0 else o[:, P:S], v,
                                            pT[:, seg, 0:S] if st == 0 else pT[:, seg, S:3 * P],
                                            start=(s_ == 0 and st == 0), stop=not nsa and st == 1,
                                            skip_group_check=True)
                        if nsa:
                            ins = pe.matmul(o[:, s_ * P:(s_ + 1) * P], vcc[0:NC, a, :], pT[0:NC, seg, 3 * P:4 * P],
                                            start=False, stop=(s_ == 1), skip_group_check=True)
                ins.then_inc(o_ps, 1)

            def latent_kv(i, n_done):
                for a in range(2):
                    pe.wait_ge(uk_in[2 * a], 16 * n_done)
                    pe.wait_ge(uk_in[2 * a + 1], 16 * n_done)
                    for c in range(LAT // P):
                        pe.matmul(att[:, 2, a * S:(a + 1) * S], wuk[:, a, c, :], cT[:, c, :],
                                  start=(a == 0 and c == 0), stop=(c == 1), skip_group_check=True)
                    for st in range(T):
                        for c in range(LAT // P):
                            ins = pe.matmul(att[:, 3, (a * T + st) * HD:(a * T + st + 1) * HD],
                                            cT[:, c, st * P:(st + 1) * P], wuv[:, a, c, :],
                                            start=(a == 0 and st == 0 and c == 0), stop=(c == 1),
                                            skip_group_check=True)
                ins.then_inc(kv_ps, 1)

            for b in range(NB):
                with pe.Fori(0, 4) as i:
                    ub, it = U0 + b * 4 * UB, 4 * b
                    src = (o1, o2, o1)[b]
                    g, y = NCH % 2, (NCH + 1) % 2
                    for j in range(UB):
                        u = ub + j
                        if j == 0:
                            pe.wait_ge(chunk_out, NCH + it + i)
                        if j == QUADS:
                            pe.wait_ge(step_free, 1 + it + i)
                            if b == 2:
                                pe.wait_ge(att_free, 9)
                        pe.wait_ge(lo_done, u + 1 + i * UB)
                        wh, wl = view(whi, u % SPLIT, 4, 512), view(wlo, u % SPLIT, 4, 512)
                        for kk in range(4):
                            for t in range(T):
                                if j < QUADS:
                                    k = 4 * j + kk
                                    ins = tokens(main[g][:, t, :], k, t, wh[:, kk, :], wl[:, kk, :], k == 0, k == KT - 1)
                                else:
                                    k = 4 * (j - QUADS) + kk
                                    cols = slice(t * P, (t + 1) * P)
                                    ins = mm3(main[y][:, t, :], src[:, 0, k, cols], src[:, 1, k, cols],
                                              wh[:, kk, :], wl[:, kk, :], k == 0, k == HEADS - 1)
                        ins.then_inc(unit_used, 1)
                        if b == 0:
                            if j == 0:
                                pe.wait_ge(att_free, 1 + i)
                                scores(1 + i, True)
                            if j == 2:
                                transposes(1 + i, True)
                            if j == 4:
                                values(1 + i, True)
                        if b == 1:
                            if j == 0:
                                pe.wait_ge(att_free, 5 + i)
                                latent_kv(i, 1 + i)
                            if j == 1:
                                pe.wait_ge(kh_out, 1 + i)
                                pe.wait_ge(vh_out, 1 + i)
                                scores(5 + i, False)
                            if j == 3:
                                transposes(5 + i, False)
                            if j == 4:
                                values(5 + i, False)

            for j in range(KT // 2):
                pe.wait_ge(step_free, 13)
                if j >= 4:
                    pe.wait_ge(m_lo, j - 3)
                for kk in range(2):
                    for t in range(T):
                        k = 2 * j + kk
                        ins = pe.transpose(att[:, j % 4, (kk * T + t) * P:(kk * T + t + 1) * P],
                                           acc[:, t, k * P:(k + 1) * P], ident[:])
                ins.then_inc(m_ps, 1)
            pe.wait_ge(m_lo, KT // 2)
            for c in range(4):
                ps = main[c % 2]
                if c >= 2:
                    pe.wait_ge(out_free, c - 1)
                for q in range(QUADS):
                    u = U1 + c * QUADS + q
                    unit_ready(u)
                    wh, wl = view(whi, u % SPLIT, 4, 512), view(wlo, u % SPLIT, 4, 512)
                    for kk in range(4):
                        for t in range(T):
                            k = 4 * q + kk
                            ins = tokens(ps[:, t, :], k, t, wh[:, kk, :], wl[:, kk, :], k == 0, k == KT - 1)
                    ins.then_inc(unit_used, 1)
            moe_pe(pe)

        @block.scalar
        def _(act):
            act.dma_start(pein[:], A["cmp_pe"][0].rearrange("a l d -> (a l) d")).then_inc(pe_in, 16)
            act.dma_start(w2[:], A["cmp_w2"][0].rearrange("a m d -> m a d")).then_inc(w2_in, 16)
            act.dma_start(kvg[:], A["kv_norm_g"].to_broadcast([P, LAT])).then_inc(kvg_in, 16)
            act.dma_start(ws[:], A["gmlp_w_s"][0].rearrange("g t s -> t g s")).then_inc(ws_in, 16)
            act.wait_ge(pe_ps, 1)
            act.activation(peT[:], att[:, 0, 0:2 * CMP], ACT.Copy).then_inc(pe_out, 1)
            for j in range(KT // 2):
                act.wait_ge(x_ps, j + 1)
                act.activation(xhi[:, 2 * j:2 * j + 2, :].rearrange("p k s -> p (k s)"),
                               main[j % 4 // 2][:, j % 2, :], ACT.Copy).then_inc(x_hi, 1)

            def hi(u, slot, turn=None, n=UNIT, wait=None):
                turn = turn if turn is not None else u // RAW
                act.wait_ge(landed[slot], 16 * (turn + 1))
                if wait is not None:
                    act.wait_ge(unit_used, wait)
                act.activation(whi[:, u % SPLIT, 0:n], raw[:, slot, 0:n], ACT.Copy).then_inc(hi_done, 1)

            def hi_at(u):
                if u == 0:
                    act.wait_ge(gn_in, 16)
                hi(u, u % RAW, n=(KT * NSM if u == 0 else UNIT), wait=u - SPLIT + 1 if u >= SPLIT else None)

            def evacuate(name):
                c, u0 = chunks[name]
                act.wait_ge(unit_used, (u0 + QUADS) if name != "small" else 1)
                ps = main[c % 2]
                flat = lambda ap: ap.rearrange("p a b -> p (a b)")
                if name == "small":
                    act.activation(flat(sm[:]), ps[:, 0, 0:T * NSM], ACT.Copy).then_inc(chunk_out, 1)
                elif name == "ckv":
                    act.activation(flat(ctm[:]), ps[:, 1, :], ACT.Copy).then_inc(ach, 1)
                    act.activation(flat(qiT[:]), ps[:, 0, :], ACT.Copy).then_inc(chunk_out, 1)
                elif name == "kcvc":
                    act.activation(flat(kcT[:]), ps[:, 0, :], ACT.Copy)
                    act.activation(flat(vcT[:]), ps[:, 1, :], ACT.Copy).then_inc(chunk_out, 1)
                elif name in ("slc", "win"):
                    k_, v_ = (ksT, vs) if name == "slc" else (kwT, vw)
                    act.activation(flat(k_[:]), ps[:, 0, :], ACT.Copy)
                    act.activation(flat(v_[:]), ps[:, 1, :], ACT.Copy).then_inc(chunk_out, 1)
                elif name[0] == "q":
                    dst = qaT if name[1] == "a" else qbT
                    for j in range(2):
                        h = int(name[2]) * 4 + j * 2
                        ins = act.activation(flat(dst[:, h:h + 2, :]), ps[:, j, :], ACT.Copy, scale=HD ** -0.5)
                    ins.then_inc(chunk_out, 1)
                elif name[0] == "v":
                    for t in range(T):
                        ins = act.activation(vt[:, t, int(name[1]) * 512:(int(name[1]) + 1) * 512], ps[:, t, :],
                                             ACT.Gelu_apprx_tanh)
                    ins.then_inc(chunk_out, 1)
                else:
                    for j in range(2):
                        g = int(name[1]) * 4 + j * 2
                        ins = act.activation(flat(uT[:, g:g + 2, :]), ps[:, j, :], ACT.Gelu_apprx_tanh)
                    ins.then_inc(chunk_out, 1)

            after = {2: lambda: evacuate("small")}
            for name in chunks:
                if name not in ("small", "u1"):
                    after[last(name) + 2] = (lambda name=name: evacuate(name))

            def extra(u):
                if u == 5:
                    act.activation(sgn[:], sm[:, :, NKI:NSM], ACT.Sigmoid).then_inc(gsig, 1)
                if u == 7:
                    act.wait_ge(ach, 1)
                    act.activation(junk[:], ctm[:, 0, :], ACT.Square, accum_out=ssq[:, 0:1]).then_inc(c_ssq, 1)
                    act.wait_ge(c_ssq, 1)
                    act.activation(junk[:], ctm[:, 1, :], ACT.Square, accum_out=ssq[:, 1:2]).then_inc(c_ssq, 1)
                if u == 9:
                    act.wait_ge(c_var, 1)
                    act.activation(rstd[:], ssq[:], ACT.Sqrt).then_inc(c_std, 1)
                if u == 12:
                    for j, (a, b) in enumerate(((xpk, xpkh), (xpv, xpvh))):
                        act.wait_ge(xp_sum, j + 1)
                        act.activation(b[:], a[:], ACT.Copy).then_inc(xp_hi, 1)
                if u == last("slc") + 3:
                    act.wait_ge(c_ps, 1)
                    act.activation(cT[:].rearrange("p c s -> p (c s)"), att[:, 2, :], ACT.Copy).then_inc(c_out, 1)
                if u == w1u + 5:
                    act.wait_ge(unit_used, w1u + 4)
                    for j in range(2):
                        ins = act.activation(g1[:, j, 0:KV * NC], att[:, 3, j * 32:j * 32 + KV * NC], ACT.Gelu_apprx_tanh)
                    ins.then_inc(g1_out, 1)
                    act.dma_start(lng[:], A["gmlp_ln_g"].to_broadcast([P, W])).then_inc(late_in, 16)
                    act.dma_start(lnb[:], A["gmlp_ln_b"].to_broadcast([P, W])).then_inc(late_in, 16)
                    act.dma_start(bsb[:].rearrange("p g t -> p (g t)"),
                                  A["gmlp_b_s"].rearrange("a g t -> a (g t)").to_broadcast([P, GG * P])).then_inc(late_in, 16)
                if u == chunks["win"][1] + 3:
                    act.wait_ge(cc_ps, 1)
                    act.activation(kcc[:, 0:KV * NC], att[:, 3, 0:KV * NC], ACT.Copy).then_inc(cc_out, 1)
                    act.activation(vcc[0:NC].rearrange("p a b -> p (a b)"), att[0:NC, 3, 256:512], ACT.Copy).then_inc(cc_out, 1)
                if u == last("win") + 3:
                    for j in range(2):
                        act.wait_ge(ws_ps, j + 1)
                        act.activation(wsT[:, 4 * j:4 * j + 4, :].rearrange("p g t -> p (g t)"), att[:, j, :],
                                       ACT.Copy).then_inc(ws_out, 1)
                if u == last("v1") + 4:
                    act.wait_ge(v_var, 1)
                    act.activation(rstd[:], bag[:, :, 1], ACT.Sqrt).then_inc(v_std, 1)

            for u in range(U0):
                hi_at(u)
                if u in after:
                    after[u]()
                extra(u)
            hi_at(U0)
            evacuate("u1")
            hi_at(U0 + 1)
            act.wait_ge(mix_u, 2)
            act.activation(o1[:, 0].rearrange("p h s -> p (h s)"), mixt[:].rearrange("p g s -> p (g s)"),
                           ACT.Copy).then_inc(oc_hi, 1)

            def exps(i, n_done, nsa):
                act.wait_ge(s_max, n_done)
                for a in range(2):
                    for s_ in range(2 if nsa else 1):
                        seg = 2 * a + s_ if nsa else a
                        for q in range(T):
                            x = sP[:, seg, P:3 * P] if q else sP[:, seg, 0:P]
                            r = 4 * q + seg
                            ins = act.activation(x, x, ACT.Exp, bias=mx[:, r:r + 1], accum_out=rs[:, r:r + 1])
                        if nsa:
                            r = 8 + 2 * a + s_
                            ins = act.activation(sC[:, a, s_, 0:NC], sC[:, a, s_, 0:NC], ACT.Exp,
                                                 bias=mx[:, r:r + 1], accum_out=rs[:, r:r + 1])
                ins.then_inc(s_exp, 1)

            for b in range(NB):
                with act.Fori(0, 4) as i:
                    if b < 2:
                        for a in range(2):
                            ins = act.activation(qst[:, a, :], (qaT, qbT)[b][:, bass.ds(4 * a + i, 1), :].rearrange("p a s -> p (a s)"),
                                                 ACT.Copy)
                        ins.then_inc(q_st, 1)
                    if b == 1:
                        for a in range(2):
                            act.dma_start(wuk[:, a], A["w_uk"][0, bass.ds(4 * a + i, 1)].rearrange("a (c p) d -> p (a c) d", p=P)).then_inc(uk_in[2 * a], 16)
                            act.dma_start(wuv[:, a], A["w_uv"][0, bass.ds(4 * a + i, 1)].rearrange("a (c p) d -> p (a c) d", p=P)).then_inc(uk_in[2 * a + 1], 16)
                    for j in range(UB):
                        u = U0 + b * 4 * UB + j + 2
                        hi(u, u % RAW, turn=u // RAW + i * (UB // RAW), wait=u - 1 + i * UB)
                        if b == 0:
                            if j == 1:
                                exps(i, 1 + i, True)
                            if j == 3:
                                act.wait_ge(p_ps, 1 + i)
                                for s_ in range(4):
                                    act.activation(pT[:, s_, 0:3 * P], att[:, s_, 0:3 * P], ACT.Copy)
                                    ins = act.activation(pT[0:NC, s_, 3 * P:4 * P], att[0:NC, s_, 3 * P:4 * P], ACT.Copy)
                                ins.then_inc(p_out, 1)
                        if b == 1:
                            if j == 0:
                                act.wait_ge(kv_ps, 1 + i)
                                act.activation(khT[:].rearrange("p a s -> p (a s)"), att[:, 2, :], ACT.Copy).then_inc(kh_out, 1)
                            if j == 2:
                                exps(i, 5 + i, False)
                            if j == 3:
                                act.wait_ge(p_ps, 5 + i)
                                for s_ in range(2):
                                    ins = act.activation(pT[:, s_, 0:3 * P], att[:, s_, 0:3 * P], ACT.Copy)
                                ins.then_inc(p_out, 1)
                        if b < 2 and j == 4:
                            act.wait_ge(o_ps, 4 * b + 1 + i)
                            for a in range(2):
                                ins = act.activation((o2, o1)[b][:, 0, bass.ds(4 * a + i, 1), :].rearrange("p a s -> p (a s)"),
                                                     att[:, a, 0:S], ACT.Copy)
                            ins.then_inc(o_hi, 1)
                        if j == 3:
                            act.wait_ge(step_free, 4 * b + 1 + i)
                            for t in range(T):
                                ins = act.activation(sig[:, t, :], main[NCH % 2][:, t, :], ACT.Sigmoid)
                            ins.then_inc(chunk_out, 1)
            for j in range(KT // 2):
                act.wait_ge(m_ps, j + 1)
                act.activation(xhi[:, 2 * j:2 * j + 2, :].rearrange("p k s -> p (k s)"), att[:, j % 4, :],
                               ACT.Copy).then_inc(m_hi, 1)
            for u in range(U1 + 2, U1 + 16):
                hi_at(u)
            act_tail(act)

        @block.vector
        def _(dve):
            ch = Chain(dve, dch)
            link = ch.link
            for j in range(KT // 2):
                dve.wait_ge(x_hi, j + 1)
                dst = (slice(None), slice(2 * j, 2 * j + 2))
                dve.tensor_tensor(xlo[dst].rearrange("p k s -> p (k s)"), main[j % 4 // 2][:, j % 2, :],
                                  xhi[dst].rearrange("p k s -> p (k s)").bitcast(F32), ALU.subtract).then_inc(x_lo, 1)

            def lo(u, slot, value, n=UNIT):
                dve.wait_ge(hi_done, value)
                dve.tensor_tensor(wlo[:, u % SPLIT, 0:n], raw[:, slot, 0:n], whi[:, u % SPLIT, 0:n].bitcast(F32),
                                  ALU.subtract).then_inc(lo_done, 1)

            def lo_at(u):
                lo(u, u % RAW, u + 1, KT * NSM if u == 0 else UNIT)

            def qseg(tensor, q):
                return tensor[:, P:3 * P] if q else tensor[:, 0:P]

            def top_rounds(n):
                for _ in range(n):
                    for q in range(T):
                        link(dve.max(top8[:, q, :], qseg(score, q)))
                        link(dve.match_replace(qseg(score, q), top8[:, q, :], qseg(score, q), TAKEN))

            def extra(u):
                if u == 3:
                    dve.wait_ge(chunk_out, 1)
                    for j in range(2):
                        ins = dve.tensor_copy(kdup[:, :, j * ID:(j + 1) * ID], sm[:, :, 0:ID])
                    ins.then_inc(kd, 1)
                if u == 6:
                    dve.wait_ge(ki_ps, 1)
                    dve.tensor_copy(kiT[:], att[:, 0, 0:S]).then_inc(ki_out, 1)
                    dve.wait_ge(gsig, 1)
                    dve.wait_ge(consts, N_CONST)
                    gv = sgn[:].rearrange("p t (a i c) -> p t i a c", a=KV, c=3)
                    for q in range(T):
                        for s_ in range(2):
                            dve.tensor_copy(gall[:, :, 4 * q:4 * q + 4].rearrange("p i (a s) -> p i a s", s=2)[:, :, :, s_],
                                            gv[:, q, :, :, 1 + s_])
                        dst = gall[:, :, 8:12].rearrange("p i (a q) -> p i a q", q=2)[:, :, :, q]
                        if q == 0:
                            ins = dve.tensor_scalar(dst, gv[:, q, :, :, 0], rowok[:, 0:1], None, ALU.mult)
                        else:
                            ins = dve.tensor_copy(dst, gv[:, q, :, :, 0])
                    link(ins)
                if u == 8:
                    dve.wait_ge(c_ssq, 2)
                    dve.tensor_scalar(ssq[:], ssq[:], 1.0 / LAT, EPS, ALU.mult, ALU.add).then_inc(c_var, 1)
                if u == 9:
                    dve.wait_ge(ix_ps, 1)
                    for h in range(IH):
                        dst = score if h == 0 else rel[:, h % 2, :]
                        for q in range(T):
                            link(dve.tensor_scalar(qseg(dst, q), qseg(att[:, h, :], q), 0.0,
                                                   sm[:, q, ID + h:ID + h + 1], ALU.max, ALU.mult))
                        if h:
                            ins = dve.tensor_tensor(score[:], score[:], rel[:, h % 2, :], ALU.add)
                            if h == IH - 1:
                                ins.then_inc(ix_sum, 1)
                            else:
                                link(ins)
                if u == 10:
                    dve.wait_ge(c_std, 1)
                    link(dve.reciprocal(rstd[:], rstd[:]))
                    dve.wait_ge(kvg_in, 16)
                    for t in range(T):
                        dve.scalar_tensor_tensor(ctm[:, t, :], ctm[:, t, :], rstd[:, t:t + 1], kvg[:], ALU.mult,
                                                 ALU.mult).then_inc(c_norm, 1)
                if u == 11:
                    dve.wait_ge(chunk_out, 3)
                    for j, (src, dst) in enumerate(((kcT, xpk), (vcT, xpv))):
                        a = src[:]
                        base = a.ap[0]
                        for h in range(KV):
                            win = bass.AP(a.tensor, a.offset + h * S, [list(base), [1, CMP], [STRIDE, NC]])
                            emb = peT[:, j * CMP:(j + 1) * CMP].unsqueeze(2).to_broadcast([P, CMP, NC])
                            ins = dve.tensor_tensor(dst[:].rearrange("p (l h b) -> p l h b", h=KV, b=NC)[:, :, h, :],
                                                    win, emb, ALU.add)
                        ins.then_inc(xp_sum, 1)
                if u == 13:
                    for j, (a, b, c) in enumerate(((xpk, xpkh, xpkl), (xpv, xpvh, xpvl))):
                        dve.wait_ge(xp_hi, j + 1)
                        dve.tensor_tensor(c[:], a[:], b[:].bitcast(F32), ALU.subtract).then_inc(xp_lo, 1)
                if u == 14:
                    dve.wait_ge(ix_mask, 2)
                if 14 <= u < 18:
                    top_rounds(2)
                if u == 18:
                    assert TOPK == 64
                    link(dve.tensor_scalar(ddsa[:], score[:], TAKEN, NEG, ALU.not_equal, ALU.mult))
                    link(dve.tensor_tensor(ddsa[:], ddsa[:], dist[:], ALU.add))
                if u == last("v1") + 3:
                    dve.wait_ge(chunk_out, chunks["v1"][0] + 1)
                    for t in range(T):
                        for j in range(2):
                            ins = dve.bn_stats(bst[:, t, j, :], vt[:, t, j * 512:(j + 1) * 512])
                    link(ins)
                    for t in range(T):
                        ins = dve.bn_aggr(bag[:, t, :], bst[:, t, 0:2, :].rearrange("p a b -> p (a b)"))
                    link(ins)
                    dve.tensor_scalar(bag[:, :, 1], bag[:, :, 1], EPS, None, ALU.add).then_inc(v_var, 1)
                if u == last("v1") + 5:
                    dve.wait_ge(v_std, 1)
                    link(dve.reciprocal(rstd[:], rstd[:]))
                    for t in range(T):
                        dve.tensor_scalar(vt[:, t, :], vt[:, t, :], bag[:, t, 0:1], rstd[:, t:t + 1], ALU.subtract,
                                          ALU.mult).then_inc(v_nrm, 1)
                if u == last("qb1") + 3:
                    dve.wait_ge(mix_ps, 1)
                    dve.wait_ge(late_in, 48)
                    for g in range(GG):
                        for c in range(T):
                            ins = dve.tensor_tensor(mixt[:, g, c * P:(c + 1) * P],
                                                    att[:, g // 2, (g % 2 * T + c) * P:(g % 2 * T + c + 1) * P],
                                                    bsb[:, g, :], ALU.add)
                    ins.then_inc(att_free, 1)
                if u == last("u0") + 3:
                    dve.wait_ge(att_free, 1)
                    dve.wait_ge(chunk_out, chunks["u0"][0] + 1)
                    dve.tensor_tensor(mixt[:, 0:4, :], mixt[:, 0:4, :], uT[:, 0:4, :], ALU.mult).then_inc(mix_u, 1)

            for u in range(U0):
                lo_at(u)
                extra(u)
            lo_at(U0)
            lo_at(U0 + 1)
            dve.wait_ge(chunk_out, NCH)
            dve.tensor_tensor(mixt[:, 4:8, :], mixt[:, 4:8, :], uT[:, 4:8, :], ALU.mult).then_inc(mix_u, 1)
            dve.wait_ge(oc_hi, 1)
            dve.tensor_tensor(o1[:, 1].rearrange("p h s -> p (h s)"), mixt[:].rearrange("p g s -> p (g s)"),
                              o1[:, 0].rearrange("p h s -> p (h s)").bitcast(F32), ALU.subtract).then_inc(step_free, 1)
            def softmax_in(i, n_done, nsa):
                dve.wait_ge(s_ps, n_done)
                dd = dist if nsa else ddsa
                for a in range(2):
                    sl = slopes[:, bass.ds(4 * a + i, 1)]
                    for q in range(T):
                        if nsa:
                            o = sP[:, 2 * a:2 * a + 2, P:3 * P] if q else sP[:, 2 * a:2 * a + 2, 0:P]
                            x = att[:, 2 * a:2 * a + 2, P:3 * P] if q else att[:, 2 * a:2 * a + 2, 0:P]
                            d = qseg(dd, q).unsqueeze(1).to_broadcast([P, 2, (q + 1) * P])
                            dve.scalar_tensor_tensor(sC[:, a, q, 0:NC], distc[:, q, 0:NC], sl,
                                                     att[:, 2 * a, 3 * P + q * 16:3 * P + q * 16 + NC], ALU.mult, ALU.add)
                        else:
                            o, x, d = qseg(sP[:, a, :], q), qseg(att[:, a, :], q), qseg(dd, q)
                        ins = dve.scalar_tensor_tensor(o, d, sl, x, ALU.mult, ALU.add)
                link(ins)
                ns = 4 if nsa else 2
                for q in range(T):
                    x = sP[:, 0:ns, P:3 * P] if q else sP[:, 0:ns, 0:P]
                    ins = dve.tensor_reduce(mx[:, 4 * q:4 * q + ns], x, AX.X, ALU.max, negate=True)
                if nsa:
                    ins = dve.tensor_reduce(mx[:, 8:12], sC[:, :, :, 0:NC], AX.X, ALU.max, negate=True)
                ins.then_inc(s_max, 1)

            def softmax_out(i, n_done, nsa):
                dve.wait_ge(s_exp, n_done)
                if not nsa:
                    r2 = rs[:, 0:8].rearrange("p (q s) -> p q s", q=T)[:, :, 0:2]
                    link(dve.reciprocal(r2, r2))
                else:
                    link(dve.reciprocal(rs[:], rs[:]))
                    link(dve.tensor_tensor(rs[:], rs[:], gall[:, bass.ds(i, 1), :].rearrange("p a b -> p (a b)"), ALU.mult))
                for a in range(2):
                    for s_ in range(2 if nsa else 1):
                        seg = 2 * a + s_ if nsa else a
                        for q in range(T):
                            x = sP[:, seg, P:3 * P] if q else sP[:, seg, 0:P]
                            r = 4 * q + seg
                            ins = dve.tensor_scalar(x, x, rs[:, r:r + 1], None, ALU.mult)
                        if nsa:
                            r = 8 + 2 * a + s_
                            ins = dve.tensor_scalar(sC[:, a, s_, 0:NC], sC[:, a, s_, 0:NC], rs[:, r:r + 1], None, ALU.mult)
                ins.then_inc(s_scaled, 1)

            for b in range(NB):
                per = (3, 3, 1)[b]
                with ch.loop(4, per) as i:
                    for j in range(UB):
                        u = U0 + b * 4 * UB + j + 2
                        lo(u, u % RAW, u + 1 + i * UB)
                        if b == 0:
                            if j == 0:
                                softmax_in(i, 1 + i, True)
                            if j == 2:
                                softmax_out(i, 1 + i, True)
                        if b == 1:
                            if j == 0:
                                dve.wait_ge(kv_ps, 1 + i)
                                dve.tensor_copy(vh[:].rearrange("p a t d -> p (a t d)"), att[:, 3, :]).then_inc(vh_out, 1)
                            if j == 1:
                                softmax_in(i, 5 + i, False)
                            if j == 3:
                                softmax_out(i, 5 + i, False)
                        if b < 2 and j == 4:
                            dve.wait_ge(o_hi, 4 * b + 1 + i)
                            dst = (o2, o1)[b]
                            for a in range(2):
                                ins = dve.tensor_tensor(dst[:, 1, bass.ds(4 * a + i, 1), :].rearrange("p a s -> p (a s)"), att[:, a, 0:S],
                                                        dst[:, 0, bass.ds(4 * a + i, 1), :].rearrange("p a s -> p (a s)").bitcast(F32), ALU.subtract)
                            ins.then_inc(att_free, 1)
                        if j == 5:
                            dve.wait_ge(chunk_out, NCH + 1 + 4 * b + i)
                            dve.wait_ge(unit_used, u - 1 + i * UB)
                            a_ = acc[:, :, bass.ds(i * 512, 512)]
                            y = main[(NCH + 1) % 2]
                            if b == 0:
                                dve.tensor_tensor(a_, sig[:], y[:], ALU.mult).then_inc(step_free, 1)
                            else:
                                link(dve.tensor_tensor(sig[:], sig[:], y[:], ALU.mult))
                                dve.tensor_tensor(a_, a_, sig[:], ALU.add).then_inc(step_free, 1)
            for j in range(KT // 2):
                dve.wait_ge(m_hi, j + 1)
                dst = (slice(None), slice(2 * j, 2 * j + 2))
                dve.tensor_tensor(xlo[dst].rearrange("p k s -> p (k s)"), att[:, j % 4, :],
                                  xhi[dst].rearrange("p k s -> p (k s)").bitcast(F32), ALU.subtract).then_inc(m_lo, 1)
            dve_tail(dve, link, lo_at)
            dve_moe(dve, ch)


_INS = ["x", "w_in", "cmp_w1", "cmp_w2", "cmp_pe", "w_uk", "w_uv", "kv_norm_g", "gmlp_ln_g", "gmlp_ln_b", "gmlp_w_s",
        "gmlp_b_s", "w_branch", "w_out", "ln1_g", "ln1_b", "router_group_w", "router_group_b", "router_expert_w",
        "router_expert_b", "expert_w_gate", "expert_w_up", "expert_w_down", "ln2_g", "ln2_b"]


def kernel(**inputs):
    import numpy as _np
    import concourse.bacc as _bacc
    from concourse import mybir as _mybir
    from concourse.bass_utils import run_bass_kernel_spmd as _run

    nc = _bacc.Bacc("TRN2", target_bir_lowering=False, num_devices=1, dynamic_dma_scratch_size=1024)
    arrays, args = {}, {}
    for name in _INS:
        a = _np.ascontiguousarray(inputs[name])
        arrays[f"in_{name}_dram"] = a
        args[name] = nc.dram_tensor(f"in_{name}_dram", a.shape, _mybir.dt.from_np(a.dtype), kind="ExternalInput").ap()
    out = nc.dram_tensor("out_dram", (1, S, D), _mybir.dt.float32, kind="ExternalOutput").ap()
    build(nc, args, out)
    r = _run(nc, [arrays], core_ids=[0])
    return r.results[0]["out_dram"]
```

```python
from contextlib import ExitStack, contextmanager

import numpy as np

import concourse.bass as bass
from concourse import mybir

F32, F32R, I32 = mybir.dt.float32, mybir.dt.float32r, mybir.dt.int32
ALU, ACT, AX = mybir.AluOpType, mybir.ActivationFunctionType, mybir.AxisListType

P = 128
D = 2048
S = 256
T = S // P
KT = D // P
HEADS, KV, HD = 8, 2, 128
GROUP = HEADS // KV
CMP, STRIDE = 32, 16
NC = (S - CMP) // STRIDE + 1
LAT = 256
IH, ID = 4, 64
TOPK = min(256, S // 4)
GG = 8
W = 1024
NB = 3
NG, EG = 4, 4
NE = NG * EG
DE = 512
SLOTS = 64
PASSES = -(-S // SLOTS)
PAIRS = NE // 2
RC = 32
MRAW = 16
MU = 24
ALPHA = 2 ** 0.25
EPS = 1e-5
NEG = -1e30
TAKEN = -3e38

C_QA, C_KC, C_KS, C_KW, C_GN = 0, 1024, 1536, 2048, 2560
C_QB, C_CKV, C_QI, C_KI, C_UV, C_GM = 2584, 3608, 3864, 4120, 4188, 6236
LB = 4
NKI = ID + IH
NGN = HEADS * 3
NSM = NKI + NGN

UNIT = 2048
RAW, SPLIT = 6, 2
QUADS = KT // 4


class Chain:

    def __init__(self, eng, sem):
        self.eng, self.sem, self.n, self.off = eng, sem, 0, 0

    def link(self, ins):
        self.n += 1
        ins.then_inc(self.sem, 1)
        self.eng.wait_ge(self.sem, self.off + self.n)

    @contextmanager
    def loop(self, count, per):
        with self.eng.Fori(0, count) as i:
            n0, off0 = self.n, self.off
            self.off = off0 + i * per
            yield i
            assert self.n - n0 == per, (self.n - n0, per)
            self.off = off0
        self.n = n0 + per * count


def build(nc, A, out):
    offset = [1152]
    made = {}

    def at(name, off, shape, dt=F32):
        return nc.alloc_sbuf_tensor_at(name, shape, dt, offset=off)

    def sb(name, shape, dt=F32):
        size = -(-int(np.prod(shape[1:])) * 4 // 32) * 32
        off = offset[0]
        offset[0] += size
        assert offset[0] <= 229344, (name, offset[0])
        made[name] = off
        return at(name, off, shape, dt)

    with ExitStack() as ctx:
        def sem(name):
            return ctx.enter_context(nc.semaphore(name))

        w_in = A["w_in"][0]
        units = []

        def chunk_units(c0):
            for q in range(QUADS):
                src = w_in[q * 512:(q + 1) * 512, c0:c0 + 512].rearrange("(k p) n -> p k n", p=P)
                units.append((src, 4, 512))

        units.append((w_in[:, C_KI:C_KI + NKI].rearrange("(k p) n -> p k n", p=P), KT, NSM))
        chunks = {"small": (0, 0)}

        def chunk(name, c0):
            chunks[name] = (len(chunks), len(units))
            chunk_units(c0)

        chunk("ckv", C_CKV)
        chunk("kcvc", C_KC)
        chunk("slc", C_KS)
        w1u = len(units)
        for j in range(2):
            for q in range(2):
                src = A["cmp_w1"][0, j, q * 2048:(q + 1) * 2048, :].rearrange("(l p) m -> p l m", p=P)
                units.append((src, 16, P))
        chunk("win", C_KW)
        chunk("qa0", C_QA)
        chunk("qa1", C_QA + 512)
        chunk("v0", C_UV + W)
        chunk("v1", C_UV + W + 512)
        chunk("qb0", C_QB)
        chunk("qb1", C_QB + 512)
        chunk("u0", C_UV)
        chunk("u1", C_UV + 512)
        U0 = len(units)
        NCH = len(chunks)
        UB = QUADS + 2
        BR = [2, 0, 1]
        U1 = U0 + NB * 4 * UB
        assert UB % RAW == 0 and UB % SPLIT == 0

        def last(name):
            return chunks[name][1] + QUADS - 1

        raw = sb("raw", [P, RAW, UNIT])
        whi = sb("whi", [P, SPLIT, UNIT], F32R)
        wlo = sb("wlo", [P, SPLIT, UNIT], F32R)
        xhi = sb("xhi", [P, KT, S], F32R)
        xlo = sb("xlo", [P, KT, S], F32R)
        acc = sb("acc", [P, T, D])
        o1 = sb("o1", [P, 2, HEADS, S], F32R)
        o2 = sb("o2", [P, 2, HEADS, S], F32R)
        qaT = sb("qaT", [P, HEADS, S])
        qbT = sb("qbT", [P, HEADS, S])
        ksT, kwT = sb("ksT", [P, KV, S]), sb("kwT", [P, KV, S])
        vs, vw = sb("vs", [P, T, KV * HD]), sb("vw", [P, T, KV * HD])
        cT = sb("cT", [P, LAT // P, S])
        ident = sb("ident", [P, P])
        dist = sb("dist", [P, 3 * P])
        ddsa = sb("ddsa", [P, 3 * P])
        distc = sb("distc", [P, T, NC + 1])
        slopes = sb("slopes", [P, HEADS])
        rowok = sb("rowok", [P, 1])
        gall = sb("gall", [P, GROUP, 12])
        sm = sb("sm", [P, T, NSM])
        kcc = sb("kcc", [P, KV * NC + 2])
        vcc = sb("vcc", [P, KV, HD])
        qst = sb("qst", [P, 2, S])
        sP = sb("sP", [P, 4, 3 * P])
        sC = sb("sC", [P, 2, T, NC + 1])
        pT = sb("pT", [P, 4, 512])
        khT = sb("khT", [P, 2, S])
        vh = sb("vh", [P, 2, T, HD])
        wuk = sb("wuk", [P, 2, 2, HD])
        wuv = sb("wuv", [P, 2, 2, HD])
        sig = sb("sig", [P, T, 512])
        mx, rs = sb("mx", [P, 12]), sb("rs", [P, 12])
        bst, bag = sb("bst", [P, T, 4, 6]), sb("bag", [P, T, 2])
        rstd, ssq = sb("rstd", [P, T]), sb("ssq", [P, T])

        R, O1, O2 = made["acc"], made["o1"], made["o2"]
        xin = at("xin", R, [P, T, D])
        kcT, vcT = at("kcT", R, [P, KV, S]), at("vcT", R + 2048, [P, KV, S])
        XP = CMP * KV * NC
        xpk = at("xpk", R + 4096, [P, XP])
        xpkh = at("xpkh", R + 4096 + 4 * XP, [P, XP], F32R)
        xpkl = at("xpkl", R + 4096 + 8 * XP, [P, XP], F32R)
        xpv = at("xpv", O1, [P, XP])
        xpvh = at("xpvh", O1 + 4 * XP, [P, XP], F32R)
        xpvl = at("xpvl", O1 + 8 * XP, [P, XP], F32R)
        ws = at("ws", O1 + 12288, [P, GG, P])
        lng, lnb = at("lng", O1, [P, W]), at("lnb", O1 + 4096, [P, W])
        mixt = at("mixt", R, [P, GG, S])
        wsT = at("wsT", R + 8192, [P, GG, P])
        bsb = at("bsb", R + 12288, [P, GG, P])
        uT, vt = at("uT", O2, [P, GG, S]), at("vt", O2 + 8192, [P, T, W])
        w2 = at("w2", O2, [P, 2, HD])
        pein = at("pein", O2 + 1024, [2 * CMP, HD])
        peT = at("peT", O2 + 2048, [P, 2 * CMP])
        g1 = at("g1", O2 + 3072, [P, 2, 32])
        kvg = at("kvg", made["pT"], [P, LAT])
        ctm = at("ctm", made["pT"] + 1024, [P, T, LAT])
        junk = at("junk", made["pT"] + 3072, [P, LAT])
        qiT = at("qiT", made["sP"], [P, 2, S])
        kiT = at("kiT", made["sP"] + 2048, [P, S])
        smT = at("smT", made["pT"] + 7168, [P, S])
        cs = at("cs", made["wuk"], [P, 2, LB * P])
        score = at("score", made["sig"], [P, 3 * P])
        rel = at("rel", made["pT"] + 4096, [P, 2, 3 * P])
        top8 = at("top8", made["qst"], [P, T, 8])
        sgn = at("sgn", made["qst"] + 64, [P, T, NGN])

        mhi, mlo = at("mhi", O2, [P, KT, S], F32R), at("mlo", made["qaT"], [P, KT, S], F32R)
        xr = at("xr", made["xlo"], [P, T, D])
        assert made["wuv"] + 2048 == made["khT"] + 8192 and made["sP"] == made["qst"] + 2048
        l1g, l1b = at("l1g", made["khT"], [P, D]), at("l1b", made["qst"], [P, D])
        l2g, l2b = at("l2g", made["khT"], [P, D]), at("l2b", made["qst"], [P, D])

        xT = at("xT", made["sig"], [P, 4, S])
        xg, ysb = at("xg", made["qaT"], [P, KT, 2 * SLOTS]), at("ysb", made["qbT"], [P, D])
        places = [O1, O1 + 8192, made["xhi"], made["xhi"] + 8192]
        places += [made["raw"] + (U1 + 10 + j) % RAW * 8192 for j in range(RAW)]
        places += [made["whi"], made["whi"] + 8192, made["wlo"], made["wlo"] + 8192, O2, O2 + 8192]
        mraw = [at(f"mraw{j}", o, [P, UNIT]) for j, o in enumerate(places)]
        small = [made["ksT"], made["pT"]]

        def carve(which, name, shape, dt=F32):
            off = small[which]
            small[which] += -(-int(np.prod(shape[1:])) * 4 // 32) * 32
            return at(name, off, shape, dt)

        hh, hT = carve(0, "hh", [P, DE]), carve(0, "hT", [P, DE // P, 2 * SLOTS])
        hot, cmb = carve(0, "hot", [P, T, 2 * SLOTS]), carve(0, "cmb", [P, T, 2 * SLOTS])
        bw = at("bw", made["ksT"], [P, KT, NG + NE])
        wsl, lgT = carve(0, "wsl", [P, S]), carve(0, "lgT", [P, S])
        assert small[0] <= made["ksT"] + 8192
        before, ones = carve(1, "before", [P, P]), carve(1, "ones", [P, P])
        iota64, iota4 = carve(1, "iota64", [P, SLOTS]), carve(1, "iota4", [P, NG])
        wr, br = carve(1, "wr", [P, KT, RC]), carve(1, "br", [P, NG + NE])
        lg, ein = carve(1, "lg", [P, T, NG + NE]), carve(1, "ein", [P, T, NG + NE])
        oh1, oh2 = carve(1, "oh1", [P, T, NG + NE]), carve(1, "oh2", [P, T, NG + NE])
        top1, top2, tmin = (carve(1, n, [P, T, 1 + NG]) for n in ("top1", "top2", "tmin"))
        eg, ed4 = carve(1, "eg", [P, T, NG]), carve(1, "ed4", [P, T, NG])
        ed, gp, wt1, wt2 = (carve(1, n, [P, T]) for n in ("ed", "gp", "wt1", "wt2"))
        sel, comb, pos = (carve(1, n, [P, T, NE]) for n in ("sel", "comb", "pos"))
        cnt, runs = carve(1, "cnt", [P, PASSES]), carve(1, "runs", [P, 4], I32)
        warm, tot = carve(1, "warm", [P, 4]), carve(1, "tot", [P, T, NE])
        fold = carve(1, "fold", [P, NG + NE])
        sums, gbr = carve(1, "sums", [P, 2, NG + NE]), carve(1, "gbr", [P, 2, NG + NE])
        gb, gbT = carve(1, "gb", [2 * KT, P]), carve(1, "gbT", [P, 2 * KT])
        nmr = carve(1, "nmr", [P, T])
        assert small[1] <= made["pT"] + 8192

        main = [ctx.enter_context(nc.psum_tensor(f"main{j}", [P, 2, 512], F32)) for j in range(2)]
        att = ctx.enter_context(nc.psum_tensor("att", [P, 4, 512], F32))

        def sems(names):
            return (sem(n) for n in names.split())

        landed = [sem(f"landed{j}") for j in range(RAW)]
        hi_done, lo_done, unit_used = sems("hi_done lo_done unit_used")
        chunk_out = sem("chunk_out")
        step_free = sem("step_free")
        pch, ach, dch = sems("pch ach dch")
        x_in = [sem(f"x_in{q}") for q in range(QUADS)]
        x_ps, x_hi, x_lo, consts = sems("x_ps x_hi x_lo consts")
        gn_in, pe_in, pe_ps, pe_out, w2_in, kvg_in, late_in = sems("gn_in pe_in pe_ps pe_out w2_in kvg_in late_in")
        ki_ps, ki_out, ix_ps, ix_sum, ix_mask = sems("ki_ps ki_out ix_ps ix_sum ix_mask")
        c_ssq, c_var, c_std, c_norm, c_ps, c_out = sems("c_ssq c_var c_std c_norm c_ps c_out")
        xp_sum, xp_hi, xp_lo, cs_out, g1_ps, g1_out, cc_ps, cc_out = sems("xp_sum xp_hi xp_lo cs_out g1_ps g1_out cc_ps cc_out")
        ws_in, ws_ps, ws_out, ws_ok, gsig = sems("ws_in ws_ps ws_out ws_ok gsig")
        v_var, v_std, v_nrm, v_ok, mix_ps, mix_u, oc_hi = sems("v_var v_std v_nrm v_ok mix_ps mix_u oc_hi")
        q_st, s_ps, s_max, s_exp, s_scaled = sems("q_st s_ps s_max s_exp s_scaled")
        p_ps, p_out, o_ps, o_hi, att_free = sems("p_ps p_out o_ps o_hi att_free")
        uk_in = [sem(f"uk_in{j}") for j in range(4)]
        kv_ps, kh_out, vh_out = sems("kv_ps kh_out vh_out")
        m_ps, m_hi, m_lo, xr_in, out_free = sems("m_ps m_hi m_lo xr_in out_free")
        l1_in, l1_var, l1_std, l1_mul, z_ok, acc_ok, gb_in, gb_ps, gb_out = sems(
            "l1_in l1_var l1_std l1_mul z_ok acc_ok gb_in gb_ps gb_out")
        wr_in, br_in, gw_ok, gs_ok, gs_ps, t_ps, t_out, lt_ps, lt_out, r_ps = sems(
            "wr_in br_in gw_ok gs_ok gs_ps t_ps t_out lt_ps lt_out r_ps")
        moe_const, sel_ok, eg_in, eg_out, ed_in, ed_out, pos_ps, np_ok = sems(
            "moe_const sel_ok eg_in eg_out ed_in ed_out pos_ps np_ok")
        mlanded = [sem(f"mlanded{j}") for j in range(MRAW)]
        m_used, hot_ok, cmb_ok, xg_ps, xg_out, ws_t, wsl_out = sems("m_used hot_ok cmb_ok xg_ps xg_out ws_t wsl_out")
        silu_ok, h_ok, ht_ps, ht_out, y_ps, y_out, sc_ps, sc_free = sems("silu_ok h_ok ht_ps ht_out y_ps y_out sc_ps sc_free")
        l2_in, l2_var, l2_std, l2_mul, z2_ok, centred, out_ok, out_ok_p, out_done = sems(
            "l2_in l2_var l2_std l2_mul z2_ok centred out_ok out_ok_p out_done")

        def view(tensor, slot, k, n):
            return tensor[:, slot, 0:k * n].rearrange("p (k n) -> p k n", n=n)

        def expert_unit(r, pair):
            e = pair * 2 + r % 2
            if r < 4 * QUADS:
                q, name = r // 4, ("expert_w_gate", "expert_w_up")[r % 4 // 2]
                rows = A[name][0, bass.ds(e, 1), q * 512:(q + 1) * 512, :]
                return rows.rearrange("a (k p) f -> p (a k) f", p=P)
            kf = (r - 4 * QUADS) // 2
            return A["expert_w_down"][0, bass.ds(e, 1), kf * P:(kf + 1) * P, :].rearrange("a p d -> p a d")

        blocks = [(n // 4, slice(n % 4 * 512, (n % 4 + 1) * 512)) for n in range(4 * T)]
        POOL_OUT, DVE_OUT = blocks[:3], blocks[3:]

        def moe_loads(sp):
            def load(r, pair, turn):
                slot = r % MRAW
                if turn is not None:
                    sp.wait_ge(m_used, turn)
                dst = mraw[slot][:]
                if r % MU < 4 * QUADS:
                    dst = dst.rearrange("p (k f) -> p k f", f=DE)
                else:
                    dst = dst.unsqueeze(1)
                sp.dma_start(dst, expert_unit(r % MU, pair)).then_inc(mlanded[slot], 16)

            def pair_of(m, r, ahead=0):
                return (m * 2 + r // MU + 2 * ahead + (PAIRS if r % MU >= 4 * QUADS else 0)) % PAIRS

            sp.wait_ge(unit_used, U1)
            for r in range(MRAW):
                if 4 <= r < 4 + RAW:
                    sp.wait_ge(lo_done, U1 + 11 + r - 4)
                if r == 4 + RAW:
                    sp.wait_ge(unit_used, U1 + 4 * QUADS)
                load(r, r // MU, None)
            sp.wait_ge(np_ok, 3)
            more = sp.value_load(runs[0:1, 2:3], min_val=PAIRS // 2 - 1, max_val=PAIRS // 2 * PASSES - 1)
            with sp.Fori(0, more) as m:
                for r in range(MRAW, 2 * MU):
                    load(r, pair_of(m, r), m * (2 * MU) + r - MRAW + 1)
                for r in range(MRAW):
                    load(r, pair_of(m, r, 1), m * (2 * MU) + 2 * MU + r - MRAW + 1)
            for r in range(MRAW, 2 * MU):
                load(r, PAIRS - 2 + r // MU, more * (2 * MU) + r - MRAW + 1)
            sp.wait_ge(acc_ok, 1)
            sp.dma_start(l2g[:], A["ln2_g"].to_broadcast([P, D])).then_inc(l2_in, 16)
            sp.dma_start(l2b[:], A["ln2_b"].to_broadcast([P, D])).then_inc(l2_in, 16)

        def moe_pe(pe, residual_T, route):
            residual_T(3)
            route(3)
            pe.wait_ge(lt_out, 1)
            for t in range(T):
                ins = pe.matmul(main[0][:, 1, t * 32:t * 32 + NG + NE], lgT[:, t * P:(t + 1) * P], fold[:],
                                start=(t == 0), stop=True, skip_group_check=True)
            ins.then_inc(r_ps, 1)
            pe.wait_ge(sel_ok, 1)
            pe.wait_ge(moe_const, 2)
            r_ = main[1][:, 0, :]
            flat = sel[:].rearrange("p t e -> p (t e)")
            pe.matmul(r_[:, 0:T * NE], before[:], flat, start=True, stop=True, skip_group_check=True)
            pe.matmul(r_[:, T * NE:2 * T * NE], ones[:], flat, start=False, stop=True,
                      skip_group_check=True).then_inc(pos_ps, 1)
            pe.wait_ge(np_ok, 1)
            pe.wait_ge(z_ok, T)
            turns = pe.value_load(runs[0:1, 0:1], min_val=PAIRS // 2, max_val=PAIRS // 2 * PASSES)

            def landed_unit(turn, r):
                pe.wait_ge(mlanded[r % MRAW], 16 * (r // MRAW + 1) + turn * (16 * (2 * MU // MRAW)))

            def step(turn, r0, m):
                def gather(q):
                    for k in range(4 * q, 4 * q + 4):
                        for t in range(T):
                            ins = pe.matmul(att[:, q, k % 4 * P:(k % 4 + 1) * P], xr[:, t, k * P:(k + 1) * P], hot[:, t, :],
                                            start=(k % 4 == 0 and t == 0), stop=(t == 1), skip_group_check=True)
                    ins.then_inc(xg_ps, 1)

                def gate_up(q):
                    pe.wait_ge(xg_out, 1 + q + m * 4)
                    for w in range(2):
                        for a in range(2):
                            landed_unit(turn, r0 + 4 * q + 2 * w + a)
                        for kk in range(4):
                            k = 4 * q + kk
                            for a in range(2):
                                unit = mraw[(r0 + 4 * q + 2 * w + a) % MRAW]
                                half = slice(a * SLOTS, (a + 1) * SLOTS)
                                ins = pe.matmul(main[0][half, w, :], xg[:, k, half], unit[:, kk * DE:(kk + 1) * DE],
                                                start=(k == 0), stop=(k == KT - 1))
                                if kk == 3:
                                    ins.then_inc(m_used, 1)

                pe.wait_ge(hot_ok, 1 + m)
                pe.wait_ge(sc_free, 1 + m * 8)
                gather(0)
                for q in range(1, QUADS):
                    gather(q)
                    if q == QUADS - 1:
                        pe.wait_ge(cmb_ok, 1 + m)
                        for t in range(T):
                            ins = pe.transpose(main[1][:, 1, t * P:(t + 1) * P], cmb[:, t, :], ident[:])
                        ins.then_inc(ws_t, 1)
                    gate_up(q - 1)
                gate_up(QUADS - 1)
                pe.wait_ge(h_ok, 1 + m)
                for f in range(DE // P):
                    ins = pe.transpose(main[1][:, 0, f * P:(f + 1) * P], hh[:, f * P:(f + 1) * P], ident[:])
                ins.then_inc(ht_ps, 1)
                pe.wait_ge(ht_out, 1 + m)
                for f in range(DE // P):
                    for a in range(2):
                        landed_unit(turn, r0 + 4 * QUADS + 2 * f + a)
                    for c in range(4):
                        for a in range(2):
                            r = r0 + 4 * QUADS + 2 * f + a
                            half = slice(a * SLOTS, (a + 1) * SLOTS)
                            ins = pe.matmul(att[half, c, :], hT[:, f, half], mraw[r % MRAW][:, c * 512:(c + 1) * 512],
                                            start=(f == 0), stop=(f == DE // P - 1))
                            if c == 3:
                                ins.then_inc(m_used, 1)
                            elif f == DE // P - 1 and a == 1:
                                ins.then_inc(y_ps, 1)
                pe.wait_ge(wsl_out, 1 + m)
                for n, (t, cols) in enumerate(blocks):
                    if t == 0:
                        pe.wait_ge(y_out, 1 + n + m * 4)
                    if n >= 2:
                        pe.wait_ge(sc_free, n + m * 8)
                    pe.matmul(main[1][:, n % 2, :], wsl[:, t * P:(t + 1) * P], ysb[:, cols],
                              start=True, stop=True).then_inc(sc_ps, 1)

            with pe.Fori(0, turns) as turn:
                for h in range(2):
                    step(turn, h * MU, turn * 2 + h)

        def act_tail(act, copy_T):
            copy_T(2)
            act.activation(warm[:, 0:1], rowok[:], ACT.Sqrt)
            copy_T(3)
            act.wait_ge(l1_var, 1)
            act.activation(rstd[:], bag[:, :, 1], ACT.Sqrt).then_inc(l1_std, 1)
            act.wait_ge(lt_ps, 1)
            act.activation(lgT[:], att[:, 3, 0:S], ACT.Copy).then_inc(lt_out, 1)
            act.wait_ge(l1_mul, 1)
            for t in range(T):
                act.activation(xr[:, t, :], xr[:, t, :], ACT.Identity, bias=nmr[:, t:t + 1],
                               scale=rstd[:, t:t + 1]).then_inc(z_ok, 1)
            act.activation(warm[:, 1:2], rowok[:], ACT.Exp)
            act.wait_ge(eg_in, 1)
            act.activation(eg[:], eg[:], ACT.Exp).then_inc(eg_out, 1)
            act.wait_ge(ed_in, 1)
            act.activation(ed[:], ed[:], ACT.Exp).then_inc(ed_out, 1)
            act.activation(warm[:, 2:3], rowok[:], ACT.Silu)
            act.wait_ge(np_ok, 2)
            steps = act.value_load(runs[0:1, 1:2], min_val=PAIRS, max_val=PAIRS * PASSES)
            with act.Fori(0, steps) as m:
                for q in range(4):
                    act.wait_ge(xg_ps, 1 + q + m * 4)
                    for k in range(4 * q, 4 * q + 4):
                        ins = act.activation(xg[:, k, :], att[:, q, k % 4 * P:(k % 4 + 1) * P], ACT.Identity,
                                             bias=gbT[:, KT + k:KT + k + 1], scale=gbT[:, k:k + 1])
                    ins.then_inc(xg_out, 1)
                act.wait_ge(ws_t, 1 + m)
                act.activation(wsl[:], main[1][:, 1, 0:S], ACT.Copy).then_inc(wsl_out, 1)
                act.wait_ge(m_used, 4 * QUADS + m * MU)
                act.activation(hh[:], main[0][:, 0, :], ACT.Silu).then_inc(silu_ok, 1)
                act.wait_ge(ht_ps, 1 + m)
                act.activation(hT[:].rearrange("p f s -> p (f s)"), main[1][:, 0, :], ACT.Copy).then_inc(ht_out, 1)
                for c in range(4):
                    if c < 3:
                        act.wait_ge(y_ps, 1 + c + m * 3)
                    else:
                        act.wait_ge(m_used, MU + m * MU)
                    act.activation(ysb[:, c * 512:(c + 1) * 512], att[:, c, :], ACT.Copy).then_inc(y_out, 1)
            act.activation(warm[:, 3:4], rowok[:], ACT.Sqrt)
            act.wait_ge(l2_var, 1)
            act.activation(rstd[:, 0:1], bag[:, 0, 1:2], ACT.Sqrt).then_inc(l2_std, 1)
            act.wait_ge(l2_mul, 1)
            for t, cols in POOL_OUT:
                act.activation(acc[:, t, cols], acc[:, t, cols], ACT.Identity, bias=nmr[:, t:t + 1],
                               scale=rstd[:, t:t + 1]).then_inc(z2_ok, 1)
            act.wait_ge(l2_var, 2)
            act.activation(rstd[:, 1:2], bag[:, 1, 1:2], ACT.Sqrt).then_inc(l2_std, 1)
            for n, (t, cols) in enumerate(POOL_OUT):
                act.wait_ge(out_ok_p, n + 1)
                act.dma_start(out[0, t * P:(t + 1) * P, cols], acc[:, t, cols]).then_inc(out_done, 16)

        def dve_moe(dve, ch):
            link = ch.link
            dve.wait_ge(r_ps, 1)
            dve.wait_ge(moe_const, 3)
            psl = main[0][:, 1, 0:64].rearrange("p (t n) -> p t n", t=T)[:, :, 0:NG + NE]
            for t in range(T):
                ins = dve.scalar_tensor_tensor(lg[:, t, :], psl[:, t, :], rstd[:, t:t + 1], ein[:, t, :], ALU.mult, ALU.add)
            link(ins)
            rows = T * (1 + NG)

            def fours(x):
                return x[:].rearrange("p t (r e) -> p (t r) e", e=4)

            def each(x):
                return x[:].rearrange("p t r -> p (t r)")

            io4 = iota4[:].unsqueeze(1).to_broadcast([P, rows, 4])

            def first_max(dst, x, top):
                link(dve.tensor_reduce(each(top), fours(x), AX.X, ALU.max))
                link(dve.tensor_tensor(fours(dst), fours(x), each(top).unsqueeze(2).to_broadcast([P, rows, 4]), ALU.is_equal))
                link(dve.tensor_tensor(fours(dst), fours(dst), io4, ALU.mult))
                link(dve.tensor_reduce(each(tmin), fours(dst), AX.X, ALU.min))
                link(dve.tensor_tensor(fours(dst), io4, each(tmin).unsqueeze(2).to_broadcast([P, rows, 4]), ALU.is_equal))

            first_max(oh1, lg, top1)
            dve.tensor_tensor(eg[:], lg[:, :, 0:NG], top1[:, :, 0:1].to_broadcast([P, T, NG]), ALU.subtract).then_inc(eg_in, 1)
            link(dve.scalar_tensor_tensor(ein[:], oh1[:], NEG, lg[:], ALU.mult, ALU.add))
            first_max(oh2, ein, top2)
            ohb = oh1[:, :, 0:NG].unsqueeze(3).to_broadcast([P, T, NG, EG])
            dve.tensor_tensor(ed4[:], top2[:, :, 1:], top1[:, :, 1:], ALU.subtract)
            link(dve.tensor_tensor(ein[:], oh1[:], oh2[:], ALU.add))
            for t in range(T):
                ins = dve.tensor_tensor(sel[:, t, :].rearrange("p (g e) -> p g e", g=NG),
                                        ein[:, t, NG:].rearrange("p (g e) -> p g e", g=NG), ohb[:, t], ALU.mult)
            ins.then_inc(sel_ok, 1)
            link(dve.tensor_tensor(ed4[:], ed4[:], oh1[:, :, 0:NG], ALU.mult))
            dve.tensor_reduce(ed[:], ed4[:], AX.X, ALU.add).then_inc(ed_in, 1)
            dve.wait_ge(pos_ps, 1)
            r_ = main[1][:, 0, :]
            tile_n = r_[:, T * NE:2 * T * NE].rearrange("p (t e) -> p t e", t=T)
            dve.tensor_copy(pos[:, 0, :], r_[:, 0:NE])
            dve.tensor_copy(pos[:, 1, :], r_[:, NE:2 * NE])
            dve.tensor_copy(tot[:], tile_n).then_inc(sc_free, 1)
            dve.wait_ge(sc_free, 1)
            dve.tensor_tensor(pos[:, 1, :], pos[:, 1, :], tot[:, 0, :], ALU.add)
            link(dve.tensor_tensor(tot[:, 0, :], tot[:, 0, :], tot[:, 1, :], ALU.add))
            link(dve.tensor_reduce(cnt[:, 0:1], tot[:, 0, :], AX.X, ALU.max))
            for c in range(1, PASSES):
                ins = dve.tensor_scalar(cnt[:, c:c + 1], cnt[:, 0:1], float(c * SLOTS), float(PAIRS), ALU.is_gt, ALU.mult)
            link(ins)
            link(dve.tensor_reduce(cnt[:, 0:1], cnt[:, 1:PASSES], AX.X, ALU.add))
            for n, (a, b) in enumerate(((0.5, PAIRS / 2), (1.0, PAIRS), (0.5, PAIRS / 2 - 1), (1.0, PAIRS - 1))):
                dve.tensor_scalar(runs[:, n:n + 1], cnt[:, 0:1], a, float(b), ALU.mult, ALU.add).then_inc(np_ok, 1)

            def slots(pair, n):
                for t in range(T):
                    for a in range(2):
                        e = bass.ds(pair * 2 + a, 1) if n is not None else slice(a, a + 1)
                        ins = dve.tensor_scalar(hot[:, t, a * SLOTS:(a + 1) * SLOTS], iota64[:], pos[:, t, e], sel[:, t, e],
                                                ALU.is_equal, ALU.mult)
                ins.then_inc(hot_ok, 1)

            def slot_weights(pair, n):
                for t in range(T):
                    for a in range(2):
                        e = bass.ds(pair * 2 + a, 1) if n is not None else slice(a, a + 1)
                        ins = dve.tensor_scalar(cmb[:, t, a * SLOTS:(a + 1) * SLOTS], iota64[:], pos[:, t, e], comb[:, t, e],
                                                ALU.is_equal, ALU.mult)
                ins.then_inc(cmb_ok, 1)
                dve.wait_ge(cmb_ok, 1 if n is None else n)
                pe_ = pos[:, :, bass.ds(pair * 2, 2) if n is not None else slice(0, 2)]
                dve.tensor_scalar(pe_, pe_, float(-SLOTS), None, ALU.add)

            slots(0, None)
            dve.wait_ge(eg_out, 1)
            link(dve.tensor_reduce(gp[:], eg[:], AX.X, ALU.add))
            link(dve.reciprocal(gp[:], gp[:]))
            dve.wait_ge(ed_out, 1)
            link(dve.tensor_scalar(wt1[:], ed[:], 1.0, None, ALU.add))
            link(dve.reciprocal(wt1[:], wt1[:]))
            link(dve.tensor_tensor(wt1[:], wt1[:], gp[:], ALU.mult))
            link(dve.tensor_tensor(wt2[:], wt1[:], ed[:], ALU.mult))
            for t in range(T):
                ins = dve.tensor_scalar(oh2[:, t, NG:], oh2[:, t, NG:], wt2[:, t:t + 1], None, ALU.mult)
            link(ins)
            for t in range(T):
                ins = dve.scalar_tensor_tensor(ein[:, t, NG:], oh1[:, t, NG:], wt1[:, t:t + 1], oh2[:, t, NG:], ALU.mult, ALU.add)
            link(ins)
            for t in range(T):
                ins = dve.tensor_tensor(comb[:, t, :].rearrange("p (g e) -> p g e", g=NG),
                                        ein[:, t, NG:].rearrange("p (g e) -> p g e", g=NG), ohb[:, t], ALU.mult)
            link(ins)
            slot_weights(0, None)
            dve.wait_ge(l1_in, 32)
            dve.wait_ge(z_ok, T)
            for t in range(T):
                ins = dve.scalar_tensor_tensor(acc[:, t, :], xr[:, t, :], ALPHA, l1g[:], ALU.mult, ALU.mult)
            link(ins)
            for t in range(T):
                ins = dve.scalar_tensor_tensor(acc[:, t, :], l1b[:], ALPHA, acc[:, t, :], ALU.mult, ALU.add)
            ins.then_inc(acc_ok, 1)
            dve.wait_ge(acc_ok, 1)
            dve.wait_ge(np_ok, 4)
            less = dve.value_load(runs[0:1, 3:4], min_val=PAIRS - 1, max_val=PAIRS * PASSES - 1)

            def combine(m, final):
                dve.wait_ge(silu_ok, 1 + m)
                dve.tensor_tensor(hh[:], hh[:], main[0][:, 1, :], ALU.mult).then_inc(h_ok, 1)
                for n, (t, cols) in enumerate(blocks):
                    dve.wait_ge(sc_ps, n + 1 + m * 8)
                    dve.tensor_tensor(acc[:, t, cols], acc[:, t, cols], main[1][:, n % 2, :], ALU.add).then_inc(sc_free, 1)
                    if final and n:
                        statistics(m, n - 1)
                    if final and n == 5:
                        variance(0)
                    if final and n == 6:
                        scale(0)

            def statistics(m, n):
                t, cols = blocks[n]
                dve.wait_ge(sc_free, n + 2 + m * 8)
                ins = dve.bn_stats(bst[:, t, n % 4, :], acc[:, t, cols])
                if n % 4 == 3:
                    link(ins)

            def variance(t):
                link(dve.bn_aggr(bag[:, t, :], bst[:, t].rearrange("p a b -> p (a b)")))
                dve.tensor_scalar(bag[:, t, 1:2], bag[:, t, 1:2], EPS, None, ALU.add).then_inc(l2_var, 1)

            def scale(t):
                dve.wait_ge(l2_std, t + 1)
                link(dve.reciprocal(rstd[:, t:t + 1], rstd[:, t:t + 1]))
                if t == 0:
                    dve.scalar_tensor_tensor(nmr[:, t:t + 1], bag[:, t, 0:1], -1.0, rstd[:, t:t + 1], ALU.mult,
                                             ALU.mult).then_inc(l2_mul, 1)

            with dve.Fori(0, less) as m:
                dve.wait_ge(ws_t, 1 + m)
                slots((m + 1) % PAIRS, m + 2)
                slot_weights((m + 1) % PAIRS, m + 2)
                combine(m, False)
            combine(less, True)
            statistics(less, 4 * T - 1)
            variance(1)
            dve.wait_ge(l2_in, 32)

            def second(n):
                t, cols = DVE_OUT[n]
                dve.wait_ge(centred, n + 1)
                dve.scalar_tensor_tensor(acc[:, t, cols], acc[:, t, cols], rstd[:, t:t + 1], l2b[:, cols], ALU.mult,
                                         ALU.add).then_inc(out_ok, 1)

            for n, (t, cols) in enumerate(DVE_OUT):
                dve.scalar_tensor_tensor(acc[:, t, cols], acc[:, t, cols], bag[:, t, 0:1], l2g[:, cols], ALU.subtract,
                                         ALU.mult).then_inc(centred, 1)
                if n == 1:
                    scale(1)
                if n:
                    second(n - 1)
            second(len(DVE_OUT) - 1)

        def dve_tail(dve, link, lo_at, merged):
            def residual(c):
                if c == 0:
                    dve.wait_ge(xr_in, 16)
                dve.wait_ge(unit_used, U1 + (c + 1) * QUADS)
                cols = slice(c * 512, (c + 1) * 512)
                for t in range(T):
                    ins = dve.scalar_tensor_tensor(xr[:, t, cols], xr[:, t, cols], ALPHA, main[(NCH + c) % 2][:, t, :],
                                                   ALU.mult, ALU.add)
                ins.then_inc(out_free, 1)
                dve.wait_ge(out_free, c + 1)
                for t in range(T):
                    ins = dve.bn_stats(bst[:, t, c, :], xr[:, t, cols])
                return ins

            for u in range(U1 + 2, U1 + 16):
                lo_at(u)
                if u == U1 + 2:
                    merged(3)
                if (u - U1 - 2) % QUADS == QUADS - 1:
                    residual((u - U1 - 2) // QUADS)
                if u == U1 + 12:
                    dve.wait_ge(gw_ok, 1)
                    dve.tensor_reduce(sums[:, 0, :], wr[:, :, 0:NG + NE].rearrange("p k n -> p n k"), AX.X, ALU.add)
                    dve.tensor_reduce(sums[:, 1, :], bw[:].rearrange("p k n -> p n k"), AX.X, ALU.add).then_inc(gs_ok, 1)
            dve.wait_ge(gs_ps, 1)
            dve.wait_ge(br_in, 32)
            tot_gb = att[:, 2, 64:64 + 2 * (NG + NE)].rearrange("p (a n) -> p a n", a=2)
            dve.tensor_copy(gbr[:, 0, :], tot_gb[:, 0, :])
            dve.tensor_tensor(gbr[:, 1, :], tot_gb[:, 1, :], br[:], ALU.add)
            ins = residual(3)
            link(ins)
            for t in range(T):
                ins = dve.bn_aggr(bag[:, t, :], bst[:, t].rearrange("p a b -> p (a b)"))
            link(ins)
            dve.tensor_scalar(bag[:, :, 1], bag[:, :, 1], EPS, None, ALU.add).then_inc(l1_var, 1)
            dve.wait_ge(l1_std, 1)
            link(dve.reciprocal(rstd[:], rstd[:]))
            dve.scalar_tensor_tensor(nmr[:], bag[:, :, 0], -1.0, rstd[:], ALU.mult, ALU.mult).then_inc(l1_mul, 1)
            dve.wait_ge(l1_mul, 1)
            for t in range(T):
                ins = dve.scalar_tensor_tensor(ein[:, t, :], gbr[:, 0, :], nmr[:, t:t + 1], gbr[:, 1, :], ALU.mult, ALU.add)
            link(ins)

        block = ctx.enter_context(nc.Block())

        @block.sync
        def _(sp):
            def load_x(q):
                cols = slice(q * 512, (q + 1) * 512)
                sp.dma_start(xin[:, :, cols], A["x"][0].rearrange("(t p) d -> p t d", p=P)[:, :, cols]).then_inc(x_in[q], 16)

            for q in range(QUADS):
                load_x(q)

            def load(u, slot, src, k, n, turn=None):
                if turn is None:
                    if u >= RAW:
                        sp.wait_ge(lo_done, u - RAW + 1)
                else:
                    sp.wait_ge(lo_done, turn)
                width = src.shape[-1]
                sp.dma_start(view(raw, slot, k, n)[:, :, 0:width], src).then_inc(landed[slot], 16)

            for u, (src, k, n) in enumerate(units):
                load(u, u % RAW, src, k, n)
                if u == 0:
                    sp.dma_start(view(raw, 0, KT, NSM)[:, :, NKI:NSM],
                                 w_in[:, C_GN:C_GN + NGN].rearrange("(k p) n -> p k n", p=P)).then_inc(gn_in, 16)
            for b, n in enumerate(BR):
                with sp.Fori(0, 4) as i:
                    for j in range(UB):
                        u = U0 + b * 4 * UB + j
                        if j < QUADS:
                            src = w_in[j * 512:(j + 1) * 512, bass.ds(C_GM + n * D + i * 512, 512)]
                        else:
                            q = j - QUADS
                            col = (i + 4) % 4 * 512
                            src = A["w_branch"][0, n, q * 512:(q + 1) * 512, bass.ds(col, 512)]
                        load(u, u % RAW, src.rearrange("(k p) n -> p k n", p=P), 4, 512,
                             turn=u - RAW + 1 + i * UB)
            for c in range(4):
                for q in range(QUADS):
                    u = U1 + c * QUADS + q
                    src = A["w_out"][0, q * 512:(q + 1) * 512, c * 512:(c + 1) * 512]
                    load(u, u % RAW, src.rearrange("(k p) n -> p k n", p=P), 4, 512)
            moe_loads(sp)
            for n, (t, cols) in enumerate(DVE_OUT):
                sp.wait_ge(out_ok, n + 1)
                sp.dma_start(out[0, t * P:(t + 1) * P, cols], acc[:, t, cols]).then_inc(out_done, 16)
            sp.wait_ge(out_done, 16 * len(blocks))

        @block.gpsimd
        def _(pool):
            ch = Chain(pool, pch)
            ch.link(pool.memset(ident[:], 0.0))
            pool.affine_select(out=ident[:], in_=ident[:], compare_op=ALU.not_equal, fill=1.0, base=0,
                               pattern=[[-1, P]], channel_multiplier=1).then_inc(consts, 1)
            for q in range(T):
                seg = dist[:, q * P:(1 + 2 * q) * P] if q else dist[:, 0:P]
                n = (q + 1) * P
                ch.link(pool.iota(seg, pattern=[[1, n]], base=-q * P, channel_multiplier=-1,
                                  allow_small_or_imprecise_dtypes=True))
                pool.affine_select(out=seg, in_=seg, compare_op=ALU.is_ge, fill=NEG, base=q * P,
                                   pattern=[[-1, n]], channel_multiplier=1).then_inc(consts, 1)
                ch.link(pool.iota(distc[:, q, 0:NC], pattern=[[STRIDE, NC]], base=CMP - 1 - q * P,
                                  channel_multiplier=-1, allow_small_or_imprecise_dtypes=True))
                pool.affine_select(out=distc[:, q, 0:NC], in_=distc[:, q, 0:NC], compare_op=ALU.is_ge, fill=NEG,
                                   base=q * P - CMP + 1, pattern=[[-STRIDE, NC]], channel_multiplier=1).then_inc(consts, 1)
            for h in range(HEADS):
                pool.memset(slopes[:, h:h + 1], 2.0 ** (-8.0 * (h + 1) / HEADS)).then_inc(consts, 1)
            ch.link(pool.memset(rowok[:], 1.0))
            pool.affine_select(out=rowok[:], in_=rowok[:], compare_op=ALU.is_ge, fill=0.0, base=1 - CMP,
                               pattern=[[0, 1]], channel_multiplier=1).then_inc(consts, 1)
            pool.wait_ge(ix_sum, 1)
            for q in range(T):
                seg = score[:, q * P:(1 + 2 * q) * P] if q else score[:, 0:P]
                pool.affine_select(out=seg, in_=seg, compare_op=ALU.is_ge, fill=NEG, base=q * P,
                                   pattern=[[-1, (q + 1) * P]], channel_multiplier=1).then_inc(ix_mask, 1)
            pool.wait_ge(ws_out, 2)
            pool.affine_select(out=wsT[:], in_=wsT[:], compare_op=ALU.is_ge, fill=0.0, base=0,
                               pattern=[[0, GG], [1, P]], channel_multiplier=-1).then_inc(ws_ok, 1)
            pool.wait_ge(late_in, 48)
            for t in range(T):
                pool.wait_ge(v_nrm, t + 1)
                ch.link(pool.tensor_tensor(vt[:, t, :], vt[:, t, :], lng[:], ALU.mult))
                pool.tensor_tensor(vt[:, t, :], vt[:, t, :], lnb[:], ALU.add).then_inc(v_ok, 1)
            pool.wait_ge(step_free, 9)
            ch.link(pool.memset(before[:], 1.0))
            pool.affine_select(out=before[:], in_=before[:], compare_op=ALU.is_ge, fill=0.0, base=-1,
                               pattern=[[1, P]], channel_multiplier=-1).then_inc(moe_const, 1)
            pool.memset(ones[:], 1.0).then_inc(moe_const, 1)
            pool.iota(iota4[:], pattern=[[1, NG]], base=-8, channel_multiplier=0, allow_small_or_imprecise_dtypes=True)
            pool.iota(iota64[:], pattern=[[1, SLOTS]], base=0, channel_multiplier=0,
                      allow_small_or_imprecise_dtypes=True).then_inc(moe_const, 1)
            ch.link(pool.tensor_copy(fold[:], ident[:, 0:NG + NE]))
            for j in range(1, P // RC):
                ch.link(pool.tensor_tensor(fold[:], fold[:], ident[:, j * RC:j * RC + NG + NE], ALU.add))
            pool.memset(wr[:, :, NG + NE:], 0.0)
            pool.wait_ge(wr_in, 32)
            pool.wait_ge(gb_out, 1)
            w_ = wr[:, :, 0:NG + NE]
            ch.link(pool.tensor_tensor(bw[:], w_, gbT[:, KT:].unsqueeze(2).to_broadcast([P, KT, NG + NE]), ALU.mult))
            pool.tensor_tensor(w_, w_, gbT[:, 0:KT].unsqueeze(2).to_broadcast([P, KT, NG + NE]), ALU.mult).then_inc(gw_ok, 1)
            pool.wait_ge(l2_in, 32)
            for n, (t, cols) in enumerate(POOL_OUT):
                pool.wait_ge(z2_ok, n + 1)
                ch.link(pool.tensor_tensor(acc[:, t, cols], acc[:, t, cols], l2g[:, cols], ALU.mult))
                pool.tensor_tensor(acc[:, t, cols], acc[:, t, cols], l2b[:, cols], ALU.add).then_inc(out_ok_p, 1)
        N_CONST = 1 + 2 * T + HEADS + 1

        @block.tensor
        def _(pe):
            pe.wait_ge(consts, 1)
            pe.wait_ge(pe_in, 16)
            pe.transpose(att[:, 0, 0:2 * CMP], pein[:], ident[0:2 * CMP, 0:2 * CMP]).then_inc(pe_ps, 1)
            for j in range(KT // 2):
                if j % 2 == 0:
                    pe.wait_ge(x_in[j // 2], 16)
                if j >= 4:
                    pe.wait_ge(x_lo, j - 3)
                bank = main[j % 4 // 2][:, j % 2, :]
                for kk in range(2):
                    for t in range(T):
                        k = 2 * j + kk
                        ins = pe.transpose(bank[:, (kk * T + t) * P:(kk * T + t + 1) * P],
                                           xin[:, t, k * P:(k + 1) * P], ident[:])
                ins.then_inc(x_ps, 1)

            def mm3(o, ah, al, bh, bl, start, stop, skip=False):
                pe.matmul(o, ah, bh, start=start, stop=False, skip_group_check=skip)
                pe.matmul(o, ah, bl, start=False, stop=False, skip_group_check=skip)
                return pe.matmul(o, al, bh, start=False, stop=stop, skip_group_check=skip)

            def tokens(o, k, t, bh, bl, start, stop, skip=False):
                cols = slice(t * P, (t + 1) * P)
                return mm3(o, xhi[:, k, cols], xlo[:, k, cols], bh, bl, start, stop, skip)

            def features(o, k, wh, wl, start, stop, skip=False):
                return mm3(o, wh, wl, xhi[:, k, :], xlo[:, k, :], start, stop, skip)

            def unit_ready(u):
                pe.wait_ge(lo_done, u + 1)

            def start_chunk(name):
                c = chunks[name][0]
                if c >= 2:
                    pe.wait_ge(chunk_out, c - 1)
                return main[c % 2], chunks[name][1]

            def feature_chunk(name, hook=None):
                ps, u0 = start_chunk(name)
                for q in range(QUADS):
                    u = u0 + q
                    unit_ready(u)
                    wh, wl = view(whi, u % SPLIT, 4, 512), view(wlo, u % SPLIT, 4, 512)
                    for kk in range(4):
                        for m in range(4):
                            k = 4 * q + kk
                            ins = features(ps[:, m // 2, m % 2 * S:(m % 2 + 1) * S], k,
                                           wh[:, kk, m * P:(m + 1) * P], wl[:, kk, m * P:(m + 1) * P],
                                           k == 0 and m % 2 == 0, k == KT - 1, True)
                    ins.then_inc(unit_used, 1)
                    if hook:
                        hook(u)

            def mixed_chunk(name, f0, t0, hook=None):
                ps, u0 = start_chunk(name)
                for q in range(QUADS):
                    u = u0 + q
                    unit_ready(u)
                    wh, wl = view(whi, u % SPLIT, 4, 512), view(wlo, u % SPLIT, 4, 512)
                    for kk in range(4):
                        k = 4 * q + kk
                        for m in range(2):
                            c = f0 + m * P
                            features(ps[:, 0, m * S:(m + 1) * S], k, wh[:, kk, c:c + P], wl[:, kk, c:c + P],
                                     k == 0 and m == 0, k == KT - 1, True)
                        for t in range(T):
                            ins = tokens(ps[:, 1, t * 256:(t + 1) * 256], k, t, wh[:, kk, t0:t0 + 256],
                                         wl[:, kk, t0:t0 + 256], k == 0 and t == 0, k == KT - 1, True)
                    ins.then_inc(unit_used, 1)
                    if hook:
                        hook(u)

            def token_chunk(name, hook=None):
                ps, u0 = start_chunk(name)
                for q in range(QUADS):
                    u = u0 + q
                    unit_ready(u)
                    wh, wl = view(whi, u % SPLIT, 4, 512), view(wlo, u % SPLIT, 4, 512)
                    for kk in range(4):
                        k = 4 * q + kk
                        for t in range(T):
                            ins = tokens(ps[:, t, :], k, t, wh[:, kk, :], wl[:, kk, :], k == 0, k == KT - 1)
                    ins.then_inc(unit_used, 1)
                    if hook:
                        hook(u)

            unit_ready(0)
            wh, wl = view(whi, 0, KT, NSM), view(wlo, 0, KT, NSM)
            for k in range(KT):
                if k % 2 == 0:
                    pe.wait_ge(x_lo, k // 2 + 1)
                ins = features(main[0][0:NSM, 0, 0:S], k, wh[:, k, :], wl[:, k, :], k == 0, k == KT - 1)
            ins.then_inc(unit_used, 1)

            def index_key(u):
                if u == last("ckv"):
                    pe.wait_ge(chunk_out, 1)
                    pe.wait_ge(pe_out, 1)
                    for t in range(T):
                        pe.transpose(att[:, 1, t * P:t * P + NSM], smT[0:NSM, t * P:(t + 1) * P], ident[0:NSM, 0:NSM])
                    for j in range(2):
                        ins = pe.matmul(att[j * ID:(j + 1) * ID, 0, 0:S], ident[0:ID, 0:ID], smT[0:ID, :],
                                        start=True, stop=True)
                    ins.then_inc(ki_ps, 1)

            mixed_chunk("ckv", 256, 0, index_key)

            def index_scores(u):
                if u == chunks["kcvc"][1] + 2:
                    pe.wait_ge(ki_out, 1)
                    pe.wait_ge(chunk_out, 2)
                    for h in range(IH):
                        rows = slice(h % 2 * ID, h % 2 * ID + ID)
                        for q in range(T):
                            ins = pe.matmul(att[:, h, q * P:(1 + 2 * q) * P if q else P],
                                            qiT[rows, h // 2, q * P:(q + 1) * P], kiT[rows, 0:(q + 1) * P],
                                            start=(q == 0), stop=True, skip_group_check=True)
                    ins.then_inc(ix_ps, 1)

            feature_chunk("kcvc", index_scores)

            def latent_T(u):
                if u == last("slc"):
                    pe.wait_ge(c_norm, T)
                    pe.wait_ge(ix_sum, 1)
                    for c in range(LAT // P):
                        for t in range(T):
                            ins = pe.transpose(att[:, 2, (c * T + t) * P:(c * T + t + 1) * P],
                                               ctm[:, t, c * P:(c + 1) * P], ident[:])
                    ins.then_inc(c_ps, 1)

            mixed_chunk("slc", 0, 256, latent_T)

            for j, (xh, xl) in enumerate(((xpkh, xpkl), (xpvh, xpvl))):
                pe.wait_ge(xp_lo, j + 1)
                for q in range(2):
                    u = w1u + 2 * j + q
                    unit_ready(u)
                    wh, wl = view(whi, u % SPLIT, 16, P), view(wlo, u % SPLIT, 16, P)
                    for l in range(0, 16, LB):
                        cols = slice((q * 16 + l) * KV * NC, (q * 16 + l + LB) * KV * NC)
                        ins = mm3(att[0:LB * KV * NC, 3 - 2 * j, :], xh[:, cols], xl[:, cols],
                                  wh[:, l:l + LB, :].rearrange("p l m -> p (l m)"),
                                  wl[:, l:l + LB, :].rearrange("p l m -> p (l m)"), q == 0 and l == 0,
                                  q == 1 and l == 16 - LB)
                    ins.then_inc(unit_used, 1)

            def compress2(u):
                if u == chunks["win"][1]:
                    pe.wait_ge(cs_out, 1)
                    n = KV * NC
                    for j in range(2):
                        for l in range(LB):
                            ins = pe.matmul(att[:, 3, j * 32:j * 32 + n], cs[0:LB * n, j, l * P:(l + 1) * P],
                                            ident[0:LB * n, l * n:(l + 1) * n], start=(j == 0 and l == 0),
                                            stop=(l == LB - 1), skip_group_check=True)
                    ins.then_inc(g1_ps, 1)
                if u == last("win"):
                    pe.wait_ge(g1_out, 1)
                    pe.wait_ge(w2_in, 16)
                    pe.matmul(att[:, 3, 0:KV * NC], w2[:, 0, :], g1[:, 0, 0:KV * NC], start=True, stop=True)
                    for h in range(KV):
                        ins = pe.matmul(att[0:NC, 3, 256 + h * HD:256 + (h + 1) * HD],
                                        g1[:, 1, h * NC:(h + 1) * NC], w2[:, 1, :], start=True, stop=True)
                    ins.then_inc(cc_ps, 1)
                if u == last("win"):
                    pe.wait_ge(ws_in, 16)
                    for g in range(GG):
                        ins = pe.transpose(att[:, g // 4, g % 4 * P:(g % 4 + 1) * P], ws[:, g, :], ident[:])
                        if g % 4 == 3:
                            ins.then_inc(ws_ps, 1)

            mixed_chunk("win", 0, 256, compress2)
            feature_chunk("qa0")
            feature_chunk("qa1")
            token_chunk("v0")
            token_chunk("v1")
            feature_chunk("qb0")

            def spatial(u):
                if u == last("qb1"):
                    pe.wait_ge(v_ok, T)
                    pe.wait_ge(ws_ok, 1)
                    pe.wait_ge(c_out, 1)
                    pe.wait_ge(cc_out, 2)
                    for g in range(GG):
                        for c in range(T):
                            ins = pe.matmul(att[:, g // 2, (g % 2 * T + c) * P:(g % 2 * T + c + 1) * P],
                                            vt[:, c, g * HD:(g + 1) * HD], wsT[:, g, :], start=True, stop=True,
                                            skip_group_check=True)
                    ins.then_inc(mix_ps, 1)

            feature_chunk("qb1", spatial)
            feature_chunk("u0")
            feature_chunk("u1")

            def scores(n_done, nsa):
                pe.wait_ge(q_st, n_done)
                for a in range(2):
                    for s_, kT in enumerate((ksT, kwT) if nsa else (khT,)):
                        bank = att[:, 2 * a + s_, :] if nsa else att[:, a, :]
                        for q in range(T):
                            ins = pe.matmul(bank[:, P:3 * P] if q else bank[:, 0:P], qst[:, a, q * P:(q + 1) * P],
                                            kT[:, a, 0:(q + 1) * P], start=(q == 0), stop=True,
                                            skip_group_check=True)
                            if nsa and s_ == 1:
                                ins = pe.matmul(att[:, 2 * a, 3 * P + q * 16:3 * P + q * 16 + NC],
                                                qst[:, a, q * P:(q + 1) * P], kcc[:, a * NC:(a + 1) * NC],
                                                start=False, stop=True, skip_group_check=True)
                ins.then_inc(s_ps, 1)

            def transposes(n_done, nsa):
                pe.wait_ge(s_scaled, n_done)
                for a in range(2):
                    for s_ in range(2 if nsa else 1):
                        seg = 2 * a + s_ if nsa else a
                        for blk in range(3):
                            ins = pe.transpose(att[:, seg, blk * P:(blk + 1) * P], sP[:, seg, blk * P:(blk + 1) * P], ident[:])
                        if nsa:
                            ins = pe.transpose(att[0:NC, seg, 3 * P:4 * P], sC[:, a, s_, 0:NC], ident[:])
                ins.then_inc(p_ps, 1)

            def values(n_done, nsa):
                pe.wait_ge(p_out, n_done)
                for a in range(2):
                    o = att[:, a, 0:S]
                    for s_ in range(2 if nsa else 1):
                        seg = 2 * a + s_ if nsa else a
                        for st in range(T):
                            if nsa:
                                v = (vs, vw)[s_][:, st, a * HD:(a + 1) * HD]
                            else:
                                v = vh[:, a, st, :]
                            ins = pe.matmul(o if st == 0 else o[:, P:S], v,
                                            pT[:, seg, 0:S] if st == 0 else pT[:, seg, S:3 * P],
                                            start=(s_ == 0 and st == 0), stop=not nsa and st == 1,
                                            skip_group_check=True)
                        if nsa:
                            ins = pe.matmul(o[:, s_ * P:(s_ + 1) * P], vcc[0:NC, a, :], pT[0:NC, seg, 3 * P:4 * P],
                                            start=False, stop=(s_ == 1), skip_group_check=True)
                ins.then_inc(o_ps, 1)

            def latent_kv(i, n_done):
                for a in range(2):
                    pe.wait_ge(uk_in[2 * a], 16 * n_done)
                    pe.wait_ge(uk_in[2 * a + 1], 16 * n_done)
                    for c in range(LAT // P):
                        pe.matmul(att[:, 2, a * S:(a + 1) * S], wuk[:, a, c, :], cT[:, c, :],
                                  start=(a == 0 and c == 0), stop=(c == 1), skip_group_check=True)
                    for st in range(T):
                        for c in range(LAT // P):
                            ins = pe.matmul(att[:, 3, (a * T + st) * HD:(a * T + st + 1) * HD],
                                            cT[:, c, st * P:(st + 1) * P], wuv[:, a, c, :],
                                            start=(a == 0 and st == 0 and c == 0), stop=(c == 1),
                                            skip_group_check=True)
                ins.then_inc(kv_ps, 1)

            def merged(c):
                pe.wait_ge(step_free, 10 + c)
                for j in (2 * c, 2 * c + 1):
                    if j >= 4:
                        pe.wait_ge(m_lo, j - 3)
                    for kk in range(2):
                        for t in range(T):
                            k = 2 * j + kk
                            ins = pe.transpose(att[:, j % 4, (kk * T + t) * P:(kk * T + t + 1) * P],
                                               acc[:, t, k * P:(k + 1) * P], ident[:])
                    ins.then_inc(m_ps, 1)

            def step(b, i):
                ub, it = U0 + b * 4 * UB, 4 * b
                src = (o1, o2, o1)[b]
                g, y = NCH % 2, (NCH + 1) % 2
                for j in range(UB):
                    u = ub + j
                    if j == 0:
                        pe.wait_ge(chunk_out, NCH + it + i)
                    if j == QUADS:
                        pe.wait_ge(step_free, 1 + it + i)
                        if b == 2:
                            pe.wait_ge(att_free, 9)
                    pe.wait_ge(lo_done, u + 1 + i * UB)
                    wh, wl = view(whi, u % SPLIT, 4, 512), view(wlo, u % SPLIT, 4, 512)
                    for kk in range(4):
                        for t in range(T):
                            if j < QUADS:
                                k = 4 * j + kk
                                ins = tokens(main[g][:, t, :], k, t, wh[:, kk, :], wl[:, kk, :], k == 0, k == KT - 1)
                            else:
                                k = 4 * (j - QUADS) + kk
                                cols = slice(t * P, (t + 1) * P)
                                ins = mm3(main[y][:, t, :], src[:, 0, k, cols], src[:, 1, k, cols],
                                          wh[:, kk, :], wl[:, kk, :], k == 0, k == HEADS - 1)
                    ins.then_inc(unit_used, 1)
                    if b == 0:
                        if j == 0:
                            pe.wait_ge(att_free, 1 + i)
                            scores(1 + i, True)
                        if j == 3:
                            transposes(1 + i, True)
                        if j == 4:
                            values(1 + i, True)
                    if b == 1:
                        if j == 0:
                            pe.wait_ge(att_free, 5 + i)
                            latent_kv(i, 1 + i)
                        if j == 1:
                            pe.wait_ge(kh_out, 1 + i)
                            pe.wait_ge(vh_out, 1 + i)
                            scores(5 + i, False)
                        if j == 3:
                            transposes(5 + i, False)
                        if j == 4:
                            values(5 + i, False)
                    if b == 2 and isinstance(i, int) and j < 3:
                        merged(j)

            for b in range(NB):
                with pe.Fori(0, 4 if b < 2 else 3) as i:
                    step(b, i)
            step(2, 3)

            def residual_T(c):
                pe.wait_ge(out_free, c + 1)
                if c:
                    pe.wait_ge(t_out, c)
                for kk in range(4):
                    for t in range(T):
                        k = 4 * c + kk
                        ins = pe.transpose(att[:, kk // 2, (kk % 2 * T + t) * P:(kk % 2 * T + t + 1) * P],
                                           xr[:, t, k * P:(k + 1) * P], ident[:])
                ins.then_inc(t_ps, 1)

            def route(c):
                pe.wait_ge(t_out, c + 1)
                pe.wait_ge(gw_ok, 1)
                for kk in range(4):
                    ins = pe.matmul(att[kk * RC:(kk + 1) * RC, 3, 0:S], wr[:, 4 * c + kk, :], xT[:, kk, :], start=(c == 0),
                                    stop=(c == 3), skip_group_check=True)
                if c == 3:
                    ins.then_inc(lt_ps, 1)

            pe.wait_ge(chunk_out, NCH + 12)
            for c in range(4):
                ps = main[(NCH + c) % 2]
                if c >= 2:
                    pe.wait_ge(out_free, c - 1)
                for q in range(QUADS):
                    u = U1 + c * QUADS + q
                    unit_ready(u)
                    if c == 0:
                        pe.wait_ge(m_lo, 2 * q + 2)
                    wh, wl = view(whi, u % SPLIT, 4, 512), view(wlo, u % SPLIT, 4, 512)
                    for kk in range(4):
                        for t in range(T):
                            k = 4 * q + kk
                            cols = slice(t * P, (t + 1) * P)
                            ins = mm3(ps[:, t, :], mhi[:, k, cols], mlo[:, k, cols], wh[:, kk, :], wl[:, kk, :],
                                      k == 0, k == KT - 1)
                    ins.then_inc(unit_used, 1)
                    if u == U1:
                        merged(3)
                    n = u - U1
                    if n == 4:
                        pe.wait_ge(gb_in, 32)
                        pe.transpose(att[:, 2, 0:2 * KT], gb[:], ident[0:2 * KT, 0:2 * KT]).then_inc(gb_ps, 1)
                    if n in (6, 10, 14):
                        residual_T(n // 4 - 1)
                    if n in (8, 12, 15):
                        route((n + 1) // 4 - 2)
                    if n == 13:
                        pe.wait_ge(gs_ok, 1)
                        pe.wait_ge(moe_const, 2)
                        pe.matmul(att[:, 2, 64:64 + 2 * (NG + NE)], ones[:], sums[:].rearrange("p a n -> p (a n)"), start=True,
                                  stop=True).then_inc(gs_ps, 1)
            moe_pe(pe, residual_T, route)

        @block.scalar
        def _(act):
            act.dma_start(pein[:], A["cmp_pe"][0].rearrange("a l d -> (a l) d")).then_inc(pe_in, 16)
            act.wait_ge(pe_ps, 1)
            act.activation(peT[:], att[:, 0, 0:2 * CMP], ACT.Copy).then_inc(pe_out, 1)
            def hi(u, slot, turn=None, n=UNIT, wait=None):
                turn = turn if turn is not None else u // RAW
                act.wait_ge(landed[slot], 16 * (turn + 1))
                if wait is not None:
                    act.wait_ge(unit_used, wait)
                act.activation(whi[:, u % SPLIT, 0:n], raw[:, slot, 0:n], ACT.Copy).then_inc(hi_done, 1)

            def hi_at(u):
                if u == 0:
                    act.wait_ge(gn_in, 16)
                hi(u, u % RAW, n=(KT * NSM if u == 0 else UNIT), wait=u - SPLIT + 1 if u >= SPLIT else None)

            def evacuate(name):
                c, u0 = chunks[name]
                act.wait_ge(unit_used, (u0 + QUADS) if name != "small" else 1)
                ps = main[c % 2]
                flat = lambda ap: ap.rearrange("p a b -> p (a b)")
                if name == "small":
                    act.activation(smT[0:NSM, :], ps[0:NSM, 0, 0:S], ACT.Copy).then_inc(chunk_out, 1)
                elif name == "ckv":
                    act.activation(flat(ctm[:]), ps[:, 1, :], ACT.Copy).then_inc(ach, 1)
                    act.activation(flat(qiT[:]), ps[:, 0, :], ACT.Copy).then_inc(chunk_out, 1)
                elif name == "kcvc":
                    act.activation(flat(kcT[:]), ps[:, 0, :], ACT.Copy)
                    act.activation(flat(vcT[:]), ps[:, 1, :], ACT.Copy).then_inc(chunk_out, 1)
                elif name in ("slc", "win"):
                    k_, v_ = (ksT, vs) if name == "slc" else (kwT, vw)
                    act.activation(flat(k_[:]), ps[:, 0, :], ACT.Copy)
                    act.activation(flat(v_[:]), ps[:, 1, :], ACT.Copy).then_inc(chunk_out, 1)
                elif name[0] == "q":
                    dst = qaT if name[1] == "a" else qbT
                    for j in range(2):
                        h = int(name[2]) * 4 + j * 2
                        ins = act.activation(flat(dst[:, h:h + 2, :]), ps[:, j, :], ACT.Copy, scale=HD ** -0.5)
                    ins.then_inc(chunk_out, 1)
                elif name[0] == "v":
                    for t in range(T):
                        ins = act.activation(vt[:, t, int(name[1]) * 512:(int(name[1]) + 1) * 512], ps[:, t, :],
                                             ACT.Gelu_apprx_tanh)
                    ins.then_inc(chunk_out, 1)
                else:
                    for j in range(2):
                        g = int(name[1]) * 4 + j * 2
                        ins = act.activation(flat(uT[:, g:g + 2, :]), ps[:, j, :], ACT.Gelu_apprx_tanh)
                    ins.then_inc(chunk_out, 1)

            after = {2: lambda: evacuate("small")}
            for name in chunks:
                if name not in ("small", "u1"):
                    after[last(name) + 2] = (lambda name=name: evacuate(name))

            def extra(u):
                if u == 7:
                    act.wait_ge(ki_out, 1)
                    act.activation(sgn[:], sm[:, :, NKI:NSM], ACT.Sigmoid).then_inc(gsig, 1)
                if u == 7:
                    act.wait_ge(ach, 1)
                    act.activation(junk[:], ctm[:, 0, :], ACT.Square, accum_out=ssq[:, 0:1]).then_inc(c_ssq, 1)
                    act.wait_ge(c_ssq, 1)
                    act.activation(junk[:], ctm[:, 1, :], ACT.Square, accum_out=ssq[:, 1:2]).then_inc(c_ssq, 1)
                if u == 9:
                    act.wait_ge(c_var, 1)
                    act.activation(rstd[:], ssq[:], ACT.Sqrt).then_inc(c_std, 1)
                if u == 12:
                    for j, (a, b) in enumerate(((xpk, xpkh), (xpv, xpvh))):
                        act.wait_ge(xp_sum, j + 1)
                        act.activation(b[:], a[:], ACT.Copy).then_inc(xp_hi, 1)
                if u == last("slc") + 3:
                    act.wait_ge(c_ps, 1)
                    act.activation(cT[:].rearrange("p c s -> p (c s)"), att[:, 2, :], ACT.Copy).then_inc(c_out, 1)
                if u == w1u + 5:
                    act.wait_ge(unit_used, w1u + 4)
                    for j in range(2):
                        ins = act.activation(cs[0:LB * KV * NC, j, :], att[0:LB * KV * NC, 3 - 2 * j, :], ACT.Copy)
                    ins.then_inc(cs_out, 1)
                if u == w1u + 7:
                    act.wait_ge(g1_ps, 1)
                    for j in range(2):
                        ins = act.activation(g1[:, j, 0:KV * NC], att[:, 3, j * 32:j * 32 + KV * NC], ACT.Gelu_apprx_tanh)
                    ins.then_inc(g1_out, 1)
                    act.dma_start(lng[:], A["gmlp_ln_g"].to_broadcast([P, W])).then_inc(late_in, 16)
                    act.dma_start(lnb[:], A["gmlp_ln_b"].to_broadcast([P, W])).then_inc(late_in, 16)
                    act.dma_start(bsb[:].rearrange("p g t -> p (g t)"),
                                  A["gmlp_b_s"].rearrange("a g t -> a (g t)").to_broadcast([P, GG * P])).then_inc(late_in, 16)
                if u == last("win") + 2:
                    act.wait_ge(cc_ps, 1)
                    act.activation(kcc[:, 0:KV * NC], att[:, 3, 0:KV * NC], ACT.Copy).then_inc(cc_out, 1)
                    act.activation(vcc[0:NC].rearrange("p a b -> p (a b)"), att[0:NC, 3, 256:512], ACT.Copy).then_inc(cc_out, 1)
                if u == last("win") + 3:
                    for j in range(2):
                        act.wait_ge(ws_ps, j + 1)
                        act.activation(wsT[:, 4 * j:4 * j + 4, :].rearrange("p g t -> p (g t)"), att[:, j, :],
                                       ACT.Copy).then_inc(ws_out, 1)
                if u == last("v1") + 4:
                    act.wait_ge(v_var, 1)
                    act.activation(rstd[:], bag[:, :, 1], ACT.Sqrt).then_inc(v_std, 1)

            for j in range(KT // 2):
                act.wait_ge(x_ps, j + 1)
                act.activation(xhi[:, 2 * j:2 * j + 2, :].rearrange("p k s -> p (k s)"),
                               main[j % 4 // 2][:, j % 2, :], ACT.Copy).then_inc(x_hi, 1)
            for u in range(U0):
                hi_at(u)
                if u == 0:
                    act.dma_start(w2[:], A["cmp_w2"][0].rearrange("a m d -> m a d")).then_inc(w2_in, 16)
                    act.dma_start(kvg[:], A["kv_norm_g"].to_broadcast([P, LAT])).then_inc(kvg_in, 16)
                    act.dma_start(ws[:], A["gmlp_w_s"][0].rearrange("g t s -> t g s")).then_inc(ws_in, 16)
                if u in after:
                    after[u]()
                extra(u)
            hi_at(U0)
            evacuate("u1")
            hi_at(U0 + 1)
            act.wait_ge(mix_u, 2)
            act.activation(o1[:, 0].rearrange("p h s -> p (h s)"), mixt[:].rearrange("p g s -> p (g s)"),
                           ACT.Copy).then_inc(oc_hi, 1)

            def exps(i, n_done, nsa):
                act.wait_ge(s_max, n_done)
                for a in range(2):
                    for s_ in range(2 if nsa else 1):
                        seg = 2 * a + s_ if nsa else a
                        for q in range(T):
                            x = sP[:, seg, P:3 * P] if q else sP[:, seg, 0:P]
                            r = 4 * q + seg
                            ins = act.activation(x, x, ACT.Exp, bias=mx[:, r:r + 1], accum_out=rs[:, r:r + 1])
                        if nsa:
                            r = 8 + 2 * a + s_
                            ins = act.activation(sC[:, a, s_, 0:NC], sC[:, a, s_, 0:NC], ACT.Exp,
                                                 bias=mx[:, r:r + 1], accum_out=rs[:, r:r + 1])
                ins.then_inc(s_exp, 1)

            def merged(c):
                for j in (2 * c, 2 * c + 1):
                    act.wait_ge(m_ps, j + 1)
                    act.activation(mhi[:, 2 * j:2 * j + 2, :].rearrange("p k s -> p (k s)"), att[:, j % 4, :],
                                   ACT.Copy).then_inc(m_hi, 1)

            def step(b, i):
                if b < 2:
                    for a in range(2):
                        ins = act.activation(qst[:, a, :], (qaT, qbT)[b][:, bass.ds(4 * a + i, 1), :].rearrange("p a s -> p (a s)"),
                                             ACT.Copy)
                    ins.then_inc(q_st, 1)
                if b == 1:
                    for a in range(2):
                        act.dma_start(wuk[:, a], A["w_uk"][0, bass.ds(4 * a + i, 1)].rearrange("a (c p) d -> p (a c) d", p=P)).then_inc(uk_in[2 * a], 16)
                        act.dma_start(wuv[:, a], A["w_uv"][0, bass.ds(4 * a + i, 1)].rearrange("a (c p) d -> p (a c) d", p=P)).then_inc(uk_in[2 * a + 1], 16)
                for j in range(UB):
                    u = U0 + b * 4 * UB + j + 2
                    hi(u, u % RAW, turn=u // RAW + i * (UB // RAW), wait=u - 1 + i * UB)
                    if b == 0:
                        if j == 1:
                            exps(i, 1 + i, True)
                        if j == 3:
                            act.wait_ge(p_ps, 1 + i)
                            act.activation(pT[:, :, 0:3 * P], att[:, :, 0:3 * P], ACT.Copy)
                            act.activation(pT[0:NC, :, 3 * P:4 * P], att[0:NC, :, 3 * P:4 * P],
                                           ACT.Copy).then_inc(p_out, 1)
                    if b == 1:
                        if j == 0:
                            act.wait_ge(kv_ps, 1 + i)
                            act.activation(khT[:].rearrange("p a s -> p (a s)"), att[:, 2, :], ACT.Copy).then_inc(kh_out, 1)
                        if j == 1:
                            exps(i, 5 + i, False)
                        if j == 3:
                            act.wait_ge(p_ps, 5 + i)
                            act.activation(pT[:, 0:2, 0:3 * P], att[:, 0:2, 0:3 * P], ACT.Copy).then_inc(p_out, 1)
                    if b < 2 and j == 4:
                        act.wait_ge(o_ps, 4 * b + 1 + i)
                        for a in range(2):
                            ins = act.activation((o2, o1)[b][:, 0, bass.ds(4 * a + i, 1), :].rearrange("p a s -> p (a s)"),
                                                 att[:, a, 0:S], ACT.Copy)
                        ins.then_inc(o_hi, 1)
                    if j == 3:
                        act.wait_ge(step_free, 4 * b + 1 + i)
                        for t in range(T):
                            ins = act.activation(sig[:, t, :], main[NCH % 2][:, t, :], ACT.Sigmoid)
                        ins.then_inc(chunk_out, 1)
                    if b == 2 and isinstance(i, int) and 1 <= j < 4:
                        merged(j - 1)

            for b in range(NB):
                with act.Fori(0, 4 if b < 2 else 3) as i:
                    step(b, i)
            step(2, 3)
            def copy_T(c):
                act.wait_ge(t_ps, c + 1)
                act.activation(xT[:].rearrange("p k s -> p (k s)"), att[:, 0:2, :].rearrange("p a s -> p (a s)"),
                               ACT.Copy).then_inc(t_out, 1)

            for u in range(U1 + 2, U1 + 16):
                hi_at(u)
                if u in (U1 + 8, U1 + 12):
                    copy_T((u - U1) // 4 - 2)
                if u == U1 + 2:
                    merged(3)
                    act.dma_start(xr[:], A["x"][0].rearrange("(t p) d -> p t d", p=P)).then_inc(xr_in, 16)
                    act.dma_start(l1g[:], A["ln1_g"].to_broadcast([P, D])).then_inc(l1_in, 16)
                    act.dma_start(l1b[:], A["ln1_b"].to_broadcast([P, D])).then_inc(l1_in, 16)
                    act.dma_start(gb[0:KT, :], A["ln1_g"][0].rearrange("(k p) -> k p", p=P)).then_inc(gb_in, 16)
                    act.dma_start(gb[KT:2 * KT, :], A["ln1_b"][0].rearrange("(k p) -> k p", p=P)).then_inc(gb_in, 16)
                    act.dma_start(wr[:, :, 0:NG], A["router_group_w"][0].rearrange("(k p) n -> p k n", p=P)).then_inc(wr_in, 16)
                    act.dma_start(wr[:, :, NG:NG + NE], A["router_expert_w"][0].rearrange("(k p) n -> p k n", p=P)).then_inc(wr_in, 16)
                    act.dma_start(br[:, 0:NG], A["router_group_b"].to_broadcast([P, NG])).then_inc(br_in, 16)
                    act.dma_start(br[:, NG:NG + NE], A["router_expert_b"].to_broadcast([P, NE])).then_inc(br_in, 16)
                if u == U1 + QUADS + 3:
                    act.wait_ge(gb_ps, 1)
                    act.activation(gbT[:], att[:, 2, 0:2 * KT], ACT.Copy).then_inc(gb_out, 1)
            act_tail(act, copy_T)

        @block.vector
        def _(dve):
            ch = Chain(dve, dch)
            link = ch.link
            def lo(u, slot, value, n=UNIT):
                dve.wait_ge(hi_done, value)
                dve.tensor_tensor(wlo[:, u % SPLIT, 0:n], raw[:, slot, 0:n], whi[:, u % SPLIT, 0:n].bitcast(F32),
                                  ALU.subtract).then_inc(lo_done, 1)

            def lo_at(u):
                lo(u, u % RAW, u + 1, KT * NSM if u == 0 else UNIT)

            def qseg(tensor, q):
                return tensor[:, P:3 * P] if q else tensor[:, 0:P]

            def top_rounds(n):
                for _ in range(n):
                    for q in range(T):
                        link(dve.max(top8[:, q, :], qseg(score, q)))
                        link(dve.match_replace(qseg(score, q), top8[:, q, :], qseg(score, q), TAKEN))

            def extra(u):
                if u == 6:
                    dve.wait_ge(ki_ps, 1)
                    dve.tensor_copy(kiT[:], att[:, 0, 0:S])
                    dve.tensor_copy(sm[:], att[:, 1, 0:S].rearrange("p (t c) -> p t c", t=T)[:, :, 0:NSM]).then_inc(ki_out, 1)
                    dve.wait_ge(ki_out, 1)
                if u == 8:
                    dve.wait_ge(gsig, 1)
                    dve.wait_ge(consts, N_CONST)
                    gv = sgn[:].rearrange("p t (a i c) -> p t i a c", a=KV, c=3)
                    for q in range(T):
                        for s_ in range(2):
                            dve.tensor_copy(gall[:, :, 4 * q:4 * q + 4].rearrange("p i (a s) -> p i a s", s=2)[:, :, :, s_],
                                            gv[:, q, :, :, 1 + s_])
                        dst = gall[:, :, 8:12].rearrange("p i (a q) -> p i a q", q=2)[:, :, :, q]
                        if q == 0:
                            ins = dve.tensor_scalar(dst, gv[:, q, :, :, 0], rowok[:, 0:1], None, ALU.mult)
                        else:
                            ins = dve.tensor_copy(dst, gv[:, q, :, :, 0])
                    link(ins)
                if u == 8:
                    dve.wait_ge(c_ssq, 2)
                    dve.tensor_scalar(ssq[:], ssq[:], 1.0 / LAT, EPS, ALU.mult, ALU.add).then_inc(c_var, 1)
                if u == 9:
                    dve.wait_ge(ix_ps, 1)
                    for h in range(IH):
                        dst = score if h == 0 else rel[:, h % 2, :]
                        for q in range(T):
                            link(dve.tensor_scalar(qseg(dst, q), qseg(att[:, h, :], q), 0.0,
                                                   sm[:, q, ID + h:ID + h + 1], ALU.max, ALU.mult))
                        if h:
                            ins = dve.tensor_tensor(score[:], score[:], rel[:, h % 2, :], ALU.add)
                            if h == IH - 1:
                                ins.then_inc(ix_sum, 1)
                            else:
                                link(ins)
                if u == 10:
                    dve.wait_ge(c_std, 1)
                    link(dve.reciprocal(rstd[:], rstd[:]))
                    dve.wait_ge(kvg_in, 16)
                    for t in range(T):
                        dve.scalar_tensor_tensor(ctm[:, t, :], ctm[:, t, :], rstd[:, t:t + 1], kvg[:], ALU.mult,
                                                 ALU.mult).then_inc(c_norm, 1)
                if u == 11:
                    dve.wait_ge(chunk_out, 3)
                    for j, (src, dst) in enumerate(((kcT, xpk), (vcT, xpv))):
                        a = src[:]
                        base = a.ap[0]
                        for h in range(KV):
                            win = bass.AP(a.tensor, a.offset + h * S, [list(base), [1, CMP], [STRIDE, NC]])
                            emb = peT[:, j * CMP:(j + 1) * CMP].unsqueeze(2).to_broadcast([P, CMP, NC])
                            ins = dve.tensor_tensor(dst[:].rearrange("p (l h b) -> p l h b", h=KV, b=NC)[:, :, h, :],
                                                    win, emb, ALU.add)
                        ins.then_inc(xp_sum, 1)
                if u == 13:
                    for j, (a, b, c) in enumerate(((xpk, xpkh, xpkl), (xpv, xpvh, xpvl))):
                        dve.wait_ge(xp_hi, j + 1)
                        dve.tensor_tensor(c[:], a[:], b[:].bitcast(F32), ALU.subtract).then_inc(xp_lo, 1)
                if u == 14:
                    dve.wait_ge(ix_mask, 2)
                if 19 <= u < 23:
                    top_rounds(2)
                if u == 23:
                    assert TOPK == 64
                    link(dve.tensor_scalar(ddsa[:], score[:], TAKEN, NEG, ALU.not_equal, ALU.mult))
                    link(dve.tensor_tensor(ddsa[:], ddsa[:], dist[:], ALU.add))
                if u == last("v1") + 3:
                    dve.wait_ge(chunk_out, chunks["v1"][0] + 1)
                    for t in range(T):
                        for j in range(2):
                            ins = dve.bn_stats(bst[:, t, j, :], vt[:, t, j * 512:(j + 1) * 512])
                    link(ins)
                    for t in range(T):
                        ins = dve.bn_aggr(bag[:, t, :], bst[:, t, 0:2, :].rearrange("p a b -> p (a b)"))
                    link(ins)
                    dve.tensor_scalar(bag[:, :, 1], bag[:, :, 1], EPS, None, ALU.add).then_inc(v_var, 1)
                if u == last("v1") + 5:
                    dve.wait_ge(v_std, 1)
                    link(dve.reciprocal(rstd[:], rstd[:]))
                    for t in range(T):
                        dve.tensor_scalar(vt[:, t, :], vt[:, t, :], bag[:, t, 0:1], rstd[:, t:t + 1], ALU.subtract,
                                          ALU.mult).then_inc(v_nrm, 1)
                if u == last("qb1") + 3:
                    dve.wait_ge(mix_ps, 1)
                    dve.wait_ge(late_in, 48)
                    for g in range(GG):
                        for c in range(T):
                            ins = dve.tensor_tensor(mixt[:, g, c * P:(c + 1) * P],
                                                    att[:, g // 2, (g % 2 * T + c) * P:(g % 2 * T + c + 1) * P],
                                                    bsb[:, g, :], ALU.add)
                    ins.then_inc(att_free, 1)
                if u == last("u0") + 3:
                    dve.wait_ge(att_free, 1)
                    dve.wait_ge(chunk_out, chunks["u0"][0] + 1)
                    dve.tensor_tensor(mixt[:, 0:4, :], mixt[:, 0:4, :], uT[:, 0:4, :], ALU.mult).then_inc(mix_u, 1)

            for j in range(KT // 2):
                dve.wait_ge(x_hi, j + 1)
                dst = (slice(None), slice(2 * j, 2 * j + 2))
                dve.tensor_tensor(xlo[dst].rearrange("p k s -> p (k s)"), main[j % 4 // 2][:, j % 2, :],
                                  xhi[dst].rearrange("p k s -> p (k s)").bitcast(F32), ALU.subtract).then_inc(x_lo, 1)
            for u in range(U0):
                lo_at(u)
                extra(u)
            lo_at(U0)
            dve.wait_ge(chunk_out, NCH)
            dve.tensor_tensor(mixt[:, 4:8, :], mixt[:, 4:8, :], uT[:, 4:8, :], ALU.mult).then_inc(mix_u, 1)
            lo_at(U0 + 1)
            dve.wait_ge(oc_hi, 1)
            dve.tensor_tensor(o1[:, 1].rearrange("p h s -> p (h s)"), mixt[:].rearrange("p g s -> p (g s)"),
                              o1[:, 0].rearrange("p h s -> p (h s)").bitcast(F32), ALU.subtract).then_inc(step_free, 1)
            def softmax_in(i, n_done, nsa):
                dve.wait_ge(s_ps, n_done)
                dd = dist if nsa else ddsa
                for a in range(2):
                    sl = slopes[:, bass.ds(4 * a + i, 1)]
                    for q in range(T):
                        if nsa:
                            o = sP[:, 2 * a:2 * a + 2, P:3 * P] if q else sP[:, 2 * a:2 * a + 2, 0:P]
                            x = att[:, 2 * a:2 * a + 2, P:3 * P] if q else att[:, 2 * a:2 * a + 2, 0:P]
                            d = qseg(dd, q).unsqueeze(1).to_broadcast([P, 2, (q + 1) * P])
                            dve.scalar_tensor_tensor(sC[:, a, q, 0:NC], distc[:, q, 0:NC], sl,
                                                     att[:, 2 * a, 3 * P + q * 16:3 * P + q * 16 + NC], ALU.mult, ALU.add)
                        else:
                            o, x, d = qseg(sP[:, a, :], q), qseg(att[:, a, :], q), qseg(dd, q)
                        ins = dve.scalar_tensor_tensor(o, d, sl, x, ALU.mult, ALU.add)
                link(ins)
                ns = 4 if nsa else 2
                for q in range(T):
                    x = sP[:, 0:ns, P:3 * P] if q else sP[:, 0:ns, 0:P]
                    ins = dve.tensor_reduce(mx[:, 4 * q:4 * q + ns], x, AX.X, ALU.max, negate=True)
                if nsa:
                    ins = dve.tensor_reduce(mx[:, 8:12], sC[:, :, :, 0:NC], AX.X, ALU.max, negate=True)
                ins.then_inc(s_max, 1)

            def softmax_out(i, n_done, nsa):
                dve.wait_ge(s_exp, n_done)
                if not nsa:
                    r2 = rs[:, 0:8].rearrange("p (q s) -> p q s", q=T)[:, :, 0:2]
                    link(dve.reciprocal(r2, r2))
                else:
                    link(dve.reciprocal(rs[:], rs[:]))
                    link(dve.tensor_tensor(rs[:], rs[:], gall[:, bass.ds(i, 1), :].rearrange("p a b -> p (a b)"), ALU.mult))
                for a in range(2):
                    for s_ in range(2 if nsa else 1):
                        seg = 2 * a + s_ if nsa else a
                        for q in range(T):
                            x = sP[:, seg, P:3 * P] if q else sP[:, seg, 0:P]
                            r = 4 * q + seg
                            ins = dve.tensor_scalar(x, x, rs[:, r:r + 1], None, ALU.mult)
                        if nsa:
                            r = 8 + 2 * a + s_
                            ins = dve.tensor_scalar(sC[:, a, s_, 0:NC], sC[:, a, s_, 0:NC], rs[:, r:r + 1], None, ALU.mult)
                ins.then_inc(s_scaled, 1)

            def merged(c):
                for j in (2 * c, 2 * c + 1):
                    dve.wait_ge(m_hi, j + 1)
                    dst = (slice(None), slice(2 * j, 2 * j + 2))
                    dve.tensor_tensor(mlo[dst].rearrange("p k s -> p (k s)"), att[:, j % 4, :],
                                      mhi[dst].rearrange("p k s -> p (k s)").bitcast(F32), ALU.subtract).then_inc(m_lo, 1)

            def step(b, i):
                for j in range(UB):
                    u = U0 + b * 4 * UB + j + 2
                    lo(u, u % RAW, u + 1 + i * UB)
                    if b == 0:
                        if j == 0:
                            softmax_in(i, 1 + i, True)
                        if j == 1:
                            softmax_out(i, 1 + i, True)
                    if b == 1:
                        if j == 0:
                            dve.wait_ge(kv_ps, 1 + i)
                            dve.tensor_copy(vh[:].rearrange("p a t d -> p (a t d)"), att[:, 3, :]).then_inc(vh_out, 1)
                        if j == 1:
                            softmax_in(i, 5 + i, False)
                            softmax_out(i, 5 + i, False)
                    if b < 2 and j == 4:
                        dve.wait_ge(o_hi, 4 * b + 1 + i)
                        dst = (o2, o1)[b]
                        for a in range(2):
                            ins = dve.tensor_tensor(dst[:, 1, bass.ds(4 * a + i, 1), :].rearrange("p a s -> p (a s)"), att[:, a, 0:S],
                                                    dst[:, 0, bass.ds(4 * a + i, 1), :].rearrange("p a s -> p (a s)").bitcast(F32), ALU.subtract)
                        ins.then_inc(att_free, 1)
                    if j == 5:
                        dve.wait_ge(chunk_out, NCH + 1 + 4 * b + i)
                        dve.wait_ge(unit_used, u - 1 + i * UB)
                        a_ = acc[:, :, bass.ds(i * 512, 512)]
                        y = main[(NCH + 1) % 2]
                        if b == 0:
                            dve.tensor_tensor(a_, sig[:], y[:], ALU.mult).then_inc(step_free, 1)
                        else:
                            link(dve.tensor_tensor(sig[:], sig[:], y[:], ALU.mult))
                            dve.tensor_tensor(a_, a_, sig[:], ALU.add).then_inc(step_free, 1)
                    if b == 2 and isinstance(i, int) and 1 <= j < 4:
                        merged(j - 1)

            for b in range(NB):
                with ch.loop(4 if b < 2 else 3, (3, 3, 1)[b]) as i:
                    step(b, i)
            step(2, 3)
            dve_tail(dve, link, lo_at, merged)
            dve_moe(dve, ch)


_INS = ["x", "w_in", "cmp_w1", "cmp_w2", "cmp_pe", "w_uk", "w_uv", "kv_norm_g", "gmlp_ln_g", "gmlp_ln_b", "gmlp_w_s",
        "gmlp_b_s", "w_branch", "w_out", "ln1_g", "ln1_b", "router_group_w", "router_group_b", "router_expert_w",
        "router_expert_b", "expert_w_gate", "expert_w_up", "expert_w_down", "ln2_g", "ln2_b"]


def kernel(**inputs):
    import numpy as _np
    import concourse.bacc as _bacc
    from concourse import mybir as _mybir
    from concourse.bass_utils import run_bass_kernel_spmd as _run

    nc = _bacc.Bacc("TRN2", target_bir_lowering=False, num_devices=1, dynamic_dma_scratch_size=1024)
    arrays, args = {}, {}
    for name in _INS:
        a = _np.ascontiguousarray(inputs[name])
        arrays[f"in_{name}_dram"] = a
        args[name] = nc.dram_tensor(f"in_{name}_dram", a.shape, _mybir.dt.from_np(a.dtype), kind="ExternalInput").ap()
    out = nc.dram_tensor("out_dram", (1, S, D), _mybir.dt.float32, kind="ExternalOutput").ap()
    build(nc, args, out)
    r = _run(nc, [arrays], core_ids=[0])
    return r.results[0]["out_dram"]
```
